# Optimizing a Trainium2 kernel written in Bass

```python
import jax, jax.numpy as jnp
from jax import lax
import numpy as np

D_MODEL = 2048
BATCH = 1
SEQ = 512
DEPTH = 1

CHUNK = 64
Q_BLOCK = 128
SB_HEADS = 8
SB_HEAD_DIM = 128
SB_WIDTH = SB_HEADS * SB_HEAD_DIM
SA_HEADS = 8
SA_HEAD_DIM = 128
SA_WIDTH = SA_HEADS * SA_HEAD_DIM
IDX_HEADS = 16
IDX_DIM = 64
TOPK_MAX = 256
RMS_EPS = 1e-6
IN_WIDTH = 4 * SB_WIDTH + 4 * SA_WIDTH + IDX_HEADS * IDX_DIM + IDX_DIM + IDX_HEADS + 2 * D_MODEL

kernel_name = "hybrid_stickbreak_dsa_gated_block"

def _split_points():
    sizes = [SB_WIDTH] * 4 + [SA_WIDTH] * 4 + [IDX_HEADS * IDX_DIM, IDX_DIM, IDX_HEADS, D_MODEL, D_MODEL]
    return [int(c) for c in np.cumsum(sizes)[:-1]]

def rms_norm(x, g):
    xf = x.astype(jnp.float32)
    y = xf * lax.rsqrt(jnp.mean(xf * xf, axis=-1, keepdims=True) + RMS_EPS)
    return (y * g.astype(jnp.float32)).astype(x.dtype)

def alibi_slopes(n_heads):
    return jnp.exp2(-8.0 * (jnp.arange(n_heads, dtype=jnp.float32) + 1.0) / n_heads)

def stick_breaking_attention(q, k, v):
    b, s, h, dh = q.shape
    scale = dh ** -0.5
    kpos = jnp.arange(s)

    def block(i):
        start = i * Q_BLOCK
        qb = lax.dynamic_slice_in_dim(q, start, Q_BLOCK, axis=1)
        qpos = start + jnp.arange(Q_BLOCK)
        z = jnp.einsum('bqhd,bshd->bhqs', qb, k).astype(jnp.float32) * scale
        strict = kpos[None, :] < qpos[:, None]
        log_keep = jnp.where(strict, jax.nn.log_sigmoid(-z), 0.0)
        after = lax.cumsum(log_keep, axis=3, reverse=True) - log_keep
        w = jnp.where(strict, jnp.exp(jax.nn.log_sigmoid(z) + after), 0.0)
        return jnp.einsum('bhqs,bshd->bqhd', w.astype(v.dtype), v)

    out = lax.map(block, jnp.arange(s // Q_BLOCK))
    return jnp.moveaxis(out, 0, 1).reshape(b, s, h, dh)

def indexed_sparse_attention(q, k, v, q_idx, k_idx, w_idx):
    b, s, h, dh = q.shape
    n_sel = min(TOPK_MAX, s // 4)
    kpos = jnp.arange(s)
    slopes = alibi_slopes(h)

    def block(i):
        start = i * Q_BLOCK
        qpos = start + jnp.arange(Q_BLOCK)
        visible = kpos[None, :] < (qpos[:, None] // CHUNK + 1) * CHUNK
        qi = lax.dynamic_slice_in_dim(q_idx, start, Q_BLOCK, axis=1)
        wi = lax.dynamic_slice_in_dim(w_idx, start, Q_BLOCK, axis=1).astype(jnp.float32) * IDX_HEADS ** -0.5
        dots = jnp.einsum('bqhd,bsd->bqhs', qi, k_idx).astype(jnp.float32) * IDX_DIM ** -0.5
        score = jnp.einsum('bqhs,bqh->bqs', jax.nn.relu(dots), wi)
        score = jnp.where(visible[None], score, -jnp.inf)
        top_val, top_idx = lax.top_k(score, n_sel)
        valid = jnp.isfinite(top_val)
        kg = jax.vmap(lambda kk, ii: kk[ii])(k, top_idx)
        vg = jax.vmap(lambda vv, ii: vv[ii])(v, top_idx)
        qb = lax.dynamic_slice_in_dim(q, start, Q_BLOCK, axis=1)
        logits = jnp.einsum('bqhd,bqkhd->bhqk', qb, kg).astype(jnp.float32) * dh ** -0.5
        dist = jnp.abs(qpos[None, :, None] - top_idx).astype(jnp.float32)
        logits = logits - slopes[None, :, None, None] * dist[:, None]
        logits = jnp.where(valid[:, None], logits, -jnp.inf)
        p = jax.nn.softmax(logits, axis=-1)
        return jnp.einsum('bhqk,bqkhd->bqhd', p.astype(v.dtype), vg)

    out = lax.map(block, jnp.arange(s // Q_BLOCK))
    return jnp.moveaxis(out, 0, 1).reshape(b, s, h, dh)

def setup_inputs(seed: int = 0) -> dict:
    key = jax.random.key(seed)
    ks = jax.random.split(key, 7)
    x = jax.random.normal(ks[0], (BATCH, SEQ, D_MODEL), jnp.float32)
    norm_gain = 1.0 + 0.01 * jax.random.normal(ks[1], (DEPTH, D_MODEL), jnp.float32)
    w_in = jax.random.normal(ks[2], (DEPTH, D_MODEL, IN_WIDTH), jnp.float32) * D_MODEL ** -0.5
    w_branch_sb = jax.random.normal(ks[3], (DEPTH, SB_WIDTH, D_MODEL), jnp.float32) * SB_WIDTH ** -0.5
    w_branch_sa = jax.random.normal(ks[4], (DEPTH, SA_WIDTH, D_MODEL), jnp.float32) * SA_WIDTH ** -0.5
    w_out = jax.random.normal(ks[5], (DEPTH, D_MODEL, D_MODEL), jnp.float32) * D_MODEL ** -0.5
    final_norm_gain = 1.0 + 0.01 * jax.random.normal(ks[6], (D_MODEL,), jnp.float32)
    return {"x": x, "norm_gain": norm_gain, "w_in": w_in, "w_branch_sb": w_branch_sb,
            "w_branch_sa": w_branch_sa, "w_out": w_out, "final_norm_gain": final_norm_gain}

def reference(x, norm_gain, w_in, w_branch_sb, w_branch_sa, w_out, final_norm_gain):
    b, s, _ = x.shape
    h = x
    splits = _split_points()
    for layer in range(DEPTH):
        u = rms_norm(h, norm_gain[layer])
        proj = jnp.einsum('bsd,de->bse', u, w_in[layer])
        (q_sb, k_sb, v_sb, z_sb, q_sa, k_sa, v_sa, z_sa,
         q_ix, k_ix, w_ix, g_sb, g_sa) = jnp.split(proj, splits, axis=-1)
        o_sb = stick_breaking_attention(q_sb.reshape(b, s, SB_HEADS, SB_HEAD_DIM),
                                        k_sb.reshape(b, s, SB_HEADS, SB_HEAD_DIM),
                                        v_sb.reshape(b, s, SB_HEADS, SB_HEAD_DIM))
        y_sb = jnp.einsum('bse,ed->bsd', o_sb.reshape(b, s, SB_WIDTH) * jax.nn.silu(z_sb), w_branch_sb[layer])
        o_sa = indexed_sparse_attention(q_sa.reshape(b, s, SA_HEADS, SA_HEAD_DIM),
                                        k_sa.reshape(b, s, SA_HEADS, SA_HEAD_DIM),
                                        v_sa.reshape(b, s, SA_HEADS, SA_HEAD_DIM),
                                        q_ix.reshape(b, s, IDX_HEADS, IDX_DIM), k_ix, w_ix)
        y_sa = jnp.einsum('bse,ed->bsd', o_sa.reshape(b, s, SA_WIDTH) * jax.nn.silu(z_sa), w_branch_sa[layer])
        mixed = jax.nn.sigmoid(g_sb) * y_sb + jax.nn.sigmoid(g_sa) * y_sa
        h = h + jnp.einsum('bsd,de->bse', mixed, w_out[layer])
    return rms_norm(h, final_norm_gain)


_drawn_inputs = setup_inputs


def setup_inputs(seed=0):
    import zlib

    import numpy as np

    out = dict(_drawn_inputs(seed))
    spreads = {}
    factors = {'norm_gain': 3.462, 'final_norm_gain': 5.574}
    for name, (base, spread) in spreads.items():
        noise = np.random.default_rng([zlib.crc32(name.encode()), seed]).standard_normal(out[name].shape)
        drawn = base * np.exp(spread * noise) if base else spread * noise
        out[name] = __import__('jax').numpy.asarray(drawn.astype(out[name].dtype))
    for name, factor in factors.items():
        out[name] = (out[name] * factor).astype(out[name].dtype)
    return out
```

```python
from contextlib import ExitStack

import concourse.bass as bass
from concourse import mybir

D_MODEL, SEQ = 2048, 512
HEADS, HD = 8, 128
IDX_HEADS, IDX_DIM = 16, 64
TOPK = min(256, SEQ // 4)
EPS = 1e-6
P = 128
QT = SEQ // P
KT = D_MODEL // P
CW = 512
NS = KT // 2
RING = 4
LEAD = 2
BIG = 1e30
HIDDEN, TAKEN = -3.0e38, -3.4e38

COL_SB = 0
COL_QIX = 8 * HEADS * HD
COL_KIX = COL_QIX + IDX_HEADS * IDX_DIM
KW = IDX_DIM + IDX_HEADS
COL_GATE = COL_KIX + KW

C_QIX, C_SB, C_SA, C_GATE, C_BRANCH, C_OUT, C_END = 0, 2, 10, 18, 26, 30, 34

WK = [SEQ - P * i for i in range(QT)]
OK = [sum(WK[:i]) for i in range(QT)]
WQ = [P * (i + 1) for i in range(QT)]
OQ = [sum(WQ[:i]) for i in range(QT)]
TRI = sum(WK)
SMALL = 1024


def build(nc, x, norm_gain, w_in, w_branch_sb, w_branch_sa, w_out, final_gain, out):
    F, R, I = mybir.dt.float32, mybir.dt.float32r, mybir.dt.int32
    ALU, ACT, AX = mybir.AluOpType, mybir.ActivationFunctionType, mybir.AxisListType
    ds = bass.ds

    place = {}

    def at(name, shape, dt, offset):
        return nc.alloc_sbuf_tensor_at(name, [P] + shape, dt, offset=offset)

    top = [(nc.sbuf_base + 31) // 32 * 32]

    def region(name, size):
        place[name] = top[0]
        top[0] += size
        return place[name]

    TILE = 4 * SEQ
    region("u_hi", KT * TILE)
    region("u_lo", KT * TILE)
    region("area", 32 * TILE)
    region("stage", 2 * 2 * TILE)
    region("w_hi", RING * 2 * TILE)
    region("w_lo", RING * 2 * TILE)
    work = region("work", 11 * TILE + 2 * 4 * TRI)
    region("far", 4 * TRI)
    region("const", 5 * 4 * P)
    region("small", SMALL)
    assert top[0] <= nc.sbuf_usable_end, top[0]

    u_hi = at("u_hi", [KT, SEQ], R, place["u_hi"])
    u_lo = at("u_lo", [KT, SEQ], R, place["u_lo"])
    hres = at("hres", [QT, D_MODEL], F, place["u_hi"])
    area = at("area", [32, SEQ], F, place["area"])
    area_r = at("area_r", [32, SEQ], R, place["area"])
    xs = at("xs", [QT, D_MODEL], F, place["area"])
    half = place["area"] + 16 * TILE
    ixw = at("ixw", [KT, KW], F, half)
    ixw_hi = at("ixw_hi", [KT, KW], R, half + 4 * KT * KW)
    ixw_lo = at("ixw_lo", [KT, KW], R, half + 8 * KT * KW)
    stage = at("stage", [2, 2, CW], F, place["stage"])
    w_hi = at("w_hi", [RING, 2, CW], R, place["w_hi"])
    w_lo = at("w_lo", [RING, 2, CW], R, place["w_lo"])

    qh, ql, kh, kl, vh, vl = [at(n, [SEQ], R, work + i * TILE)
                              for i, n in enumerate(["qh", "ql", "kh", "kl", "vh", "vl"])]
    x_hi = at("x_hi", [TRI], R, work + 6 * TILE)
    p_sa = at("p_sa", [TRI], F, work + 6 * TILE)
    x_lo = at("x_lo", [TRI], R, work + 6 * TILE + 4 * TRI)
    w2 = work + 6 * TILE + 8 * TRI
    full = at("full", [2, SEQ], F, w2)
    eb = at("eb", [2, SEQ], F, w2 + 2 * TILE)
    v_t = at("v_t", [SEQ], F, w2 + 3 * TILE)
    og = at("og", [SEQ], F, w2 + 4 * TILE)
    gain = at("gain", [D_MODEL], F, work)
    junk = at("junk", [D_MODEL], F, work + 4 * TILE)
    xg = at("xg", [QT, D_MODEL], F, place["w_hi"])
    kix_hi = at("kix_hi", [SEQ], R, work)
    kix_lo = at("kix_lo", [SEQ], R, work + TILE)
    kw_t = at("kw_t", [SEQ], F, work + 2 * TILE)
    relu = at("relu", [2, SEQ], F, work + 8 * TILE)
    score = at("score", [2, SEQ], F, work + 10 * TILE)
    dist_i = at("dist_i", [TRI], I, work + 3 * TILE)
    o_in = at("o_in", [HEADS, SEQ], F, work)
    mix = at("mix", [QT, SEQ], F, work + 8 * TILE)
    mix_sa = at("mix_sa", [SEQ], F, work + 12 * TILE)
    fgain = at("fgain", [D_MODEL], F, work)
    junk2 = at("junk2", [QT, CW], F, work + 4 * TILE)

    far = at("far", [TRI], F, place["far"])
    ident = at("ident", [P], F, place["const"])
    big_ident = at("big_ident", [P], R, place["const"] + 4 * P)
    neg_tri = at("neg_tri", [P], R, place["const"] + 8 * P)
    neg_one = at("neg_one", [P], R, place["const"] + 12 * P)
    before = at("before", [P], F, place["const"] + 16 * P)
    cst = at("cst", [2, P], F, w2 + 4 * TILE)

    small_at = [place["small"]]

    def small(name, shape):
        size = 4
        for d in shape:
            size *= d
        small_at[0] += (size + 31) // 32 * 32
        assert small_at[0] <= place["small"] + SMALL
        return at(name, shape, F, small_at[0] - (size + 31) // 32 * 32)

    wix = small("wix", [QT, IDX_HEADS])
    top8 = small("top8", [8])
    ss, var, root, rinv, tmp, rstd = [small(n, [QT]) for n in ("ss", "var", "root", "rinv", "tmp", "rstd")]
    nmax, psum_p, pinv = [small(n, [QT]) for n in ("nmax", "psum_p", "pinv")]
    slope = small("slope", [HEADS])
    ssq = small("ssq", [QT, 4])

    proj = [nc.alloc_psum_tensor(f"proj{i}", [P, CW], F) for i in range(4)]
    attn = [nc.alloc_psum_tensor(f"attn{i}", [P, CW], F) for i in range(4)]

    o_dram = nc.dram_tensor("o_scratch", (2 * HEADS, P, SEQ), F, kind="Internal").ap()

    win = w_in[0].rearrange("(t p) e -> p t e", p=P)
    wsb = w_branch_sb[0].rearrange("(t p) e -> p t e", p=P)
    wsa = w_branch_sa[0].rearrange("(t p) e -> p t e", p=P)
    wout = w_out[0].rearrange("(t p) e -> p t e", p=P)
    x_rows = x[0].rearrange("(i p) d -> i p d", p=P)
    out_rows = out[0].rearrange("(i p) d -> i p d", p=P)

    def sem(name):
        return nc.alloc_semaphore(name)

    strip_loaded = [sem("strip_loaded0"), sem("strip_loaded1")]
    strip_hi, strip_lo, strip_used = sem("strip_hi"), sem("strip_lo"), sem("strip_used")
    proj_done, proj_free = sem("proj_done"), sem("proj_free")
    x_loaded = [sem(f"x_loaded{i}") for i in range(QT)]
    gain_loaded, ixw_loaded, consts, masks = sem("gain_loaded"), sem("ixw_loaded"), sem("consts"), sem("masks")
    xg_ready, sumsq, norm_step, rooted, xn_ready = sem("xg_ready"), sem("sumsq"), sem("norm_step"), sem("rooted"), sem("xn_ready")
    xt_done, u_hi_ready, u_lo_ready = sem("xt_done"), sem("u_hi_ready"), sem("u_lo_ready")
    ixw_hi_ready, ixw_lo_ready, kw_done, kw_copied = sem("ixw_hi_ready"), sem("ixw_lo_ready"), sem("kw_done"), sem("kw_copied")
    kix_hi_ready, kix_lo_ready, kix_both = sem("kix_hi_ready"), sem("kix_lo_ready"), sem("kix_both")
    wix_turned, wix_ready, dist_ready, far_ready = sem("wix_turned"), sem("wix_ready"), sem("dist_ready"), sem("far_ready")
    qix_hi_ready = sem("qix_hi_ready")
    dots_done, relu_ready, relu_used, pick_step = sem("dots_done"), sem("relu_ready"), sem("relu_used"), sem("pick_step")
    v_staged, qk_hi, qk_lo = sem("v_staged"), sem("qk_hi"), sem("qk_lo")
    v_turned, v_hi, v_lo = sem("v_turned"), sem("v_hi"), sem("v_lo")
    z_done, e_step, e_ready, sp_step, sp_ready = sem("z_done"), sem("e_step"), sem("e_ready"), sem("sp_step"), sem("sp_ready")
    sp_hi, sp_lo, c_done = sem("sp_hi"), sem("sp_lo"), sem("c_done")
    w_full, w_low, av_done = sem("w_full"), sem("w_low"), sem("av_done")
    gate_exp, silu_step, o_ready, o_stored = sem("gate_exp"), sem("silu_step"), sem("o_ready"), sem("o_stored")
    lg_ready, max_ready, p_exp, inv_ready, p_ready = sem("lg_ready"), sem("max_ready"), sem("p_exp"), sem("inv_ready"), sem("p_ready")
    pt_done, pt_hi = sem("pt_done"), sem("pt_hi")
    sigmoid_ready = sem("sigmoid_ready")
    o_loaded = [sem(f"o_loaded{i}") for i in range(4)]
    o_hi, o_lo = sem("o_hi"), sem("o_lo")
    branch_sa_done, attn_free, mix_step, mix_ready, mix_hi, mix_lo = (
        sem("branch_sa_done"), sem("attn_free"), sem("mix_step"), sem("mix_ready"), sem("mix_hi"), sem("mix_lo"))
    res_loaded, fgain_loaded, h_ready, sq_done, y_stored = (
        sem("res_loaded"), sem("fgain_loaded"), sem("h_ready"), sem("sq_done"), sem("y_stored"))
    y_ready = [sem("y_ready_even"), sem("y_ready_odd")]
    hg_ready = sem("hg_ready")

    SCALE = float(HD) ** -0.5

    def bank_done(eng, c, e, strips=NS, done=proj_done, m=None):
        if e < 3:
            eng.wait_ge(done, (c if m is None else m) * 3 + (e + 1))
        else:
            eng.wait_ge(strip_used, c * NS + strips)

    block = nc.Block()

    with block:
        @block.sync
        def _(sp):
            for i in range(QT):
                sp.dma_start(xs[:, i, :], x_rows[i]).then_inc(x_loaded[i], 16)
                if i == 0:
                    sp.dma_start(gain[:, :], norm_gain[0:1, :].to_broadcast([P, D_MODEL])
                                 ).then_inc(gain_loaded, 16)
            sp.dma_start(ixw[:, :, :], win[:, :, COL_KIX:COL_KIX + KW]).then_inc(ixw_loaded, 16)

            def load_strip(c, s, src):
                if not (isinstance(c, int) and NS * c + s < 2):
                    sp.wait_ge(strip_lo, c * NS + (s - 1))
                sp.dma_start(stage[:, s % 2, :, :], src).then_inc(strip_loaded[s % 2], 16)

            def load_chunk(c, source, col):
                for s in range(NS):
                    load_strip(c, s, source(s)[:, :, ds(col, CW)] if not isinstance(col, int)
                               else source(s)[:, :, col:col + CW])

            def rows(w):
                return lambda s: w[:, 2 * s:2 * s + 2, :]

            def branch_rows(s):
                return (wsb if s < NS // 2 else wsa)[:, 2 * (s % (NS // 2)):2 * (s % (NS // 2)) + 2, :]

            for c in range(C_QIX, C_SB):
                load_chunk(c, rows(win), COL_QIX + CW * c)
            with sp.Fori(C_SB, C_GATE) as c:
                load_chunk(c, rows(win), c * CW - C_SB * CW)
            with sp.Fori(C_GATE, C_BRANCH) as c:
                load_chunk(c, rows(win), c * CW + (COL_GATE - C_GATE * CW))
            with sp.Fori(C_BRANCH, C_OUT) as c:
                load_chunk(c, branch_rows, c * CW - C_BRANCH * CW)
            with sp.Fori(C_OUT, C_END) as c:
                load_chunk(c, rows(wout), c * CW - C_OUT * CW)
            for i in range(QT):
                sp.wait_ge(y_ready[i % 2], i // 2 + 1)
                sp.dma_start(out_rows[i], hres[:, i, :]).then_inc(y_stored, 16)
            sp.wait_ge(y_stored, 16 * QT)

        @block.gpsimd
        def _(pool):
            g = nc.gpsimd
            g.memset(ident[:, :], 0.0).then_inc(consts, 1)
            g.memset(before[:, :], 1.0).then_inc(consts, 1)
            g.memset(cst[:, 0, :], 0.0).then_inc(consts, 1)
            g.memset(cst[:, 1, :], -1.0).then_inc(consts, 1)
            pool.wait_ge(consts, 4)
            g.affine_select(out=ident[:, :], in_=ident[:, :], compare_op=ALU.not_equal, fill=1.0,
                            base=0, pattern=[[-1, P]], channel_multiplier=1).then_inc(masks, 1)
            g.affine_select(out=before[:, :], in_=before[:, :], compare_op=ALU.is_gt, fill=0.0,
                            base=0, pattern=[[1, P]], channel_multiplier=-1).then_inc(masks, 1)
            g.affine_select(out=cst[:, 0, :], in_=cst[:, 0, :], compare_op=ALU.is_gt, fill=-1.0,
                            base=0, pattern=[[1, P]], channel_multiplier=-1).then_inc(masks, 1)
            pool.wait_ge(gain_loaded, 16)
            for i in range(QT):
                pool.wait_ge(x_loaded[i], 16)
                g.tensor_tensor(xg[:, i, :], xs[:, i, :], gain[:, :], ALU.mult).then_inc(xg_ready, 1)
            pool.wait_ge(sumsq, QT)
            pool.wait_ge(xg_ready, QT)
            for i in range(QT):
                g.iota(dist_i[:, OQ[i]:OQ[i] + WQ[i]], pattern=[[-1, WQ[i]]], base=P * i,
                       channel_multiplier=1).then_inc(dist_ready, 1)
            pool.wait_ge(kix_lo_ready, 1)
            pool.dma_start(kix_hi[IDX_DIM:P, :], kix_hi[0:IDX_DIM, :]).then_inc(kix_both, 16)
            pool.dma_start(kix_lo[IDX_DIM:P, :], kix_lo[0:IDX_DIM, :]).then_inc(kix_both, 16)

            def head(hh, v_slot, store):
                g.tensor_copy(v_t[:, :], area[:, ds(v_slot, 1), :]).then_inc(v_staged, 1)
                pool.wait_ge(o_ready, hh + 1)
                pool.dma_start(store, og[:, :]).then_inc(o_stored, 16)
                pool.wait_ge(o_stored, hh * 16 + 16)

            pool.wait_ge(proj_free, 4 * C_SA)
            pool.wait_ge(far_ready, QT)
            with pool.Fori(0, HEADS) as n:
                head(n, n + 2 * HEADS, o_dram[ds(n, 1)].rearrange("a p s -> p (a s)"))
            pool.wait_ge(proj_free, 4 * C_GATE)
            with pool.Fori(0, 2) as a:
                with pool.Fori(0, 4) as b:
                    n = a * 4 + b
                    head(n + HEADS, b * 8 + a + 4, o_dram[ds(n + HEADS, 1)].rearrange("a p s -> p (a s)"))

            pool.wait_ge(av_done, 2 * HEADS)
            pool.wait_ge(o_stored, 16 * 2 * HEADS)
            for j in range(4):
                if j >= 2:
                    pool.wait_ge(o_lo, 4 * (j - 1))
                pool.dma_start(o_in[:, 4 * (j % 2):4 * (j % 2) + 4, :],
                               o_dram[4 * j:4 * j + 4].rearrange("a p s -> p a s")).then_inc(o_loaded[j], 16)
            pool.wait_ge(strip_used, NS * C_OUT)
            pool.dma_start(hres[:, :, :], x[0].rearrange("(i p) d -> p i d", p=P)).then_inc(res_loaded, 16)
            pool.dma_start(fgain[:, :], final_gain.rearrange("(a d) -> a d", a=1).to_broadcast([P, D_MODEL])
                           ).then_inc(fgain_loaded, 16)

        @block.scalar
        def _(act):
            A = nc.scalar.activation

            def split_hi(c, s):
                if isinstance(c, int) and NS * c + s >= NS * C_END:
                    return
                act.wait_ge(strip_loaded[s % 2], c * (16 * NS // 2) + 16 * (s // 2 + 1))
                if not (isinstance(c, int) and NS * c + s < RING):
                    act.wait_ge(strip_used, c * NS + (s - RING + 1))
                A(w_hi[:, s % RING, :, :], stage[:, s % 2, :, :], ACT.Copy).then_inc(strip_hi, 1)

            def chunk(c, steps=()):
                for s in range(NS):
                    split_hi(c, s + LEAD)
                    if s < len(steps) and steps[s]:
                        steps[s]()

            def apart():
                act.nop(nofuse=True)

            def evacuate(c, dst):
                for e in range(4):
                    bank_done(act, c, e)
                    apart()
                    A(dst(e), proj[e][:, :], ACT.Copy).then_inc(proj_free, 1)

            def turned_u_high(i):
                for j in range(4):
                    act.wait_ge(xt_done, 4 * i + j + 1)
                    A(u_hi[:, 4 * j:4 * j + 4, P * i:P * i + P],
                      attn[j][:, :].rearrange("p (t s) -> p t s", t=4), ACT.Copy).then_inc(u_hi_ready, 1)

            for i in range(QT):
                act.wait_ge(x_loaded[i], 16)
                if i:
                    act.wait_ge(sumsq, i)
                A(junk[:, :], xs[:, i, :], ACT.Square, accum_out=ss[:, i:i + 1]).then_inc(sumsq, 1)
                act.wait_ge(norm_step, 6 * i + 1)
                A(root[:, i:i + 1], var[:, i:i + 1], ACT.Sqrt).then_inc(rooted, 1)
                if i:
                    turned_u_high(i - 1)
            act.wait_ge(ixw_loaded, 16)
            A(ixw_hi[:, :, :], ixw[:, :, :], ACT.Copy).then_inc(ixw_hi_ready, 1)
            turned_u_high(QT - 1)
            act.wait_ge(xt_done, 4 * QT)
            for s in range(LEAD):
                split_hi(0, s)
            act.wait_ge(kw_done, 1)
            A(kix_hi[0:IDX_DIM, :], proj[3][0:IDX_DIM, :], ACT.Copy).then_inc(kix_hi_ready, 1)
            A(kw_t[0:KW, :], proj[3][0:KW, :], ACT.Copy).then_inc(kw_copied, 1)
            act.wait_ge(dist_ready, QT)
            A(far[:, :], dist_i[:, :], ACT.Abs).then_inc(far_ready, 1)

            nc.scalar.preload_act_table_set("natural_log_exp_and_others")
            for c in range(C_QIX, C_SB):
                chunk(c)
                for e in range(4):
                    bank_done(act, c, e)
                    A(area_r[:, 16 + 4 * c + e, :], proj[e][:, :], ACT.Copy).then_inc(qix_hi_ready, 1)

            def relu_step(qi, s):
                def f():
                    for h in (2 * s, 2 * s + 1):
                        n = IDX_HEADS * (qi - 1) + h
                        act.wait_ge(dots_done, n + 1)
                        if n >= 2:
                            act.wait_ge(relu_used, n - 1)
                        A(relu[:, n % 2, 0:WQ[qi]], attn[h % 4][:, 0:WQ[qi]], ACT.Relu).then_inc(relu_ready, 1)
                return f

            for c in range(C_SB, C_SB + 4):
                qi = c - C_SB + 1
                chunk(c, [relu_step(qi, s) for s in range(NS - 1)] if qi < QT else ())
                evacuate(c, lambda e: area[:, 4 * (c - C_SB) + e, :])
                if qi < QT:
                    relu_step(qi, NS - 1)()
            with act.Fori(C_SB + 4, C_SA) as c:
                chunk(c)
                evacuate(c, lambda e: area[:, ds(c * 4 + (e - 4 * C_SB), 1), :])

            def stage_qk(hh, q_slot, k_slot):
                def f():
                    act.wait_ge(strip_used, hh * NS + (NS * C_SA - NS + 3))
                    apart()
                    A(qh[:, :], area[:, ds(q_slot, 1), :], ACT.Copy, scale=SCALE).then_inc(qk_hi, 1)
                    A(kh[:, :], area[:, ds(k_slot, 1), :], ACT.Copy).then_inc(qk_hi, 1)
                return f

            def v_high(hh):
                act.wait_ge(v_turned, hh + 1)
                A(vh[:, :], attn[3][:, :], ACT.Copy).then_inc(v_hi, 1)

            def gate_exp_z(hh, z_slot):
                act.wait_ge(v_staged, hh + 1)
                apart()
                A(og[:, :], area[:, ds(z_slot, 1), :], ACT.Exp, scale=-1.0).then_inc(gate_exp, 1)

            def sb_steps(n):
                def e_tile(i):
                    w = WK[i]
                    act.wait_ge(z_done, n * 4 + i + 1)
                    if i >= 2:
                        act.wait_ge(sp_ready, n * 4 + i - 1)
                    t = eb[:, i % 2, 0:w]
                    A(t, attn[i][:, 0:w], ACT.Abs).then_inc(e_step, 1)
                    act.wait_ge(e_step, n * 8 + 2 * i + 1)
                    A(t, t, ACT.Exp, scale=-1.0).then_inc(e_step, 1)
                    act.wait_ge(e_step, n * 8 + 2 * i + 2)
                    A(t, t, ACT.Ln, bias=1.0).then_inc(e_ready, 1)

                def sp_high(i):
                    act.wait_ge(sp_ready, n * 4 + i + 1)
                    A(x_hi[:, OK[i]:OK[i] + WK[i]], full[:, i % 2, 0:WK[i]], ACT.Copy).then_inc(sp_hi, 1)

                def weights(i):
                    w = WK[i]
                    if i == 0:
                        act.wait_ge(c_done, n * 4 + 4)
                    if i >= 2:
                        act.wait_ge(w_low, n * 4 + i - 1)
                    A(full[:, i % 2, 0:w], attn[i][:, 0:w], ACT.Exp).then_inc(w_full, 1)
                    A(x_hi[:, OK[i]:OK[i] + w], attn[i][:, 0:w], ACT.Exp).then_inc(w_full, 1)

                def s1():
                    v_high(n)
                    e_tile(0)
                    e_tile(1)

                def s2():
                    sp_high(0)
                    e_tile(2)
                    sp_high(1)

                def s3():
                    e_tile(3)
                    sp_high(2)
                    sp_high(3)

                def s5():
                    weights(0)
                    weights(1)

                def s6():
                    weights(2)
                    weights(3)

                return [stage_qk(n, n, n + HEADS), s1, s2, s3,
                        lambda: gate_exp_z(n, n + 3 * HEADS), s5, s6]

            with act.Fori(0, HEADS) as n:
                c = n + C_SA
                chunk(c, sb_steps(n))
                act.wait_ge(v_staged, n + 1)
                act.wait_ge(qk_lo, n * 2 + 2)
                act.wait_ge(silu_step, n * 3 + 3)
                evacuate(c, lambda e: area[:, ds(n + 8 * e, 1), :])

            def sa_steps(n, slot):
                hh = n + HEADS

                def probs(i):
                    act.wait_ge(max_ready, n * 4 + i + 1)
                    t = p_sa[:, OQ[i]:OQ[i] + WQ[i]]
                    A(t, t, ACT.Exp, bias=nmax[:, i:i + 1],
                      accum_out=psum_p[:, i:i + 1]).then_inc(p_exp, 1)

                def turned_high(i):
                    if i == 0:
                        act.wait_ge(pt_done, n * 4 + 4)
                    A(x_hi[:, OK[i]:OK[i] + WK[i]], attn[i][:, 0:WK[i]], ACT.Copy).then_inc(pt_hi, 1)

                def s2():
                    probs(0)
                    probs(1)

                def s3():
                    probs(2)
                    probs(3)

                def s5():
                    for i in range(QT):
                        turned_high(i)

                return [stage_qk(hh, slot(0), slot(1)), lambda: v_high(hh), s2, s3,
                        lambda: gate_exp_z(hh, slot(3)), s5]

            with act.Fori(0, 2) as a:
                with act.Fori(0, 4) as b:
                    n = a * 4 + b
                    chunk(n + C_GATE, sa_steps(n, lambda kind: b * 8 + a + 2 * kind))
                    act.wait_ge(v_staged, n + HEADS + 1)
                    act.wait_ge(qk_lo, n * 2 + 2 * HEADS + 2)
                    act.wait_ge(silu_step, n * 3 + 3 * HEADS + 3)
                    evacuate(n + C_GATE, lambda e: area[:, ds(b * 8 + a + 2 * e, 1), :])

            def o_high(ts):
                def f():
                    for t in ts:
                        if t % 4 == 0:
                            act.wait_ge(o_loaded[t // 4], 16)
                        if t == 0:
                            act.wait_ge(strip_used, NS * C_BRANCH)
                        A(u_hi[:, t, :], o_in[:, t % HEADS, :], ACT.Copy).then_inc(o_hi, 1)
                return f

            def sigmoid_steps(c):
                def f(e):
                    def g():
                        t = area[:, 8 * (c - C_BRANCH) + 2 * e:8 * (c - C_BRANCH) + 2 * e + 2, :] \
                            if isinstance(c, int) else area[:, ds(c * 8 + (2 * e - 8 * C_BRANCH), 2), :]
                        A(t, t, ACT.Sigmoid).then_inc(sigmoid_ready, 1)
                    return g
                return [f(e) for e in range(4)]

            def mix_high(c):
                for e in range(4):
                    d = c * 4 + (e - 4 * C_BRANCH)
                    act.wait_ge(mix_ready, d + 1)
                    apart()
                    A(area_r[:, ds(d * 2, 1), :], mix[:, e, :], ACT.Copy).then_inc(mix_hi, 1)

            o_high(range(0, 8))()
            chunk(C_BRANCH, [o_high(range(8, 12)), o_high(range(12, 16))] + sigmoid_steps(C_BRANCH))
            for e in range(4):
                act.wait_ge(mix_ready, e + 1)
                A(area_r[:, 2 * e, :], mix[:, e, :], ACT.Copy).then_inc(mix_hi, 1)
            with act.Fori(C_BRANCH + 1, C_OUT) as c:
                chunk(c, sigmoid_steps(c))
                mix_high(c)

            def squares(c):
                m = c - C_OUT
                for i in range(QT):
                    act.wait_ge(h_ready, m * 4 + i + 1)
                    src = hres[:, i, CW * m:CW * m + CW] if isinstance(c, int) else hres[:, i, ds(m * CW, CW)]
                    acc = ssq[:, i, m:m + 1] if isinstance(c, int) else ssq[:, i, ds(m, 1)]
                    if m:
                        act.wait_ge(sq_done, m * 4 + i - 3)
                    A(junk2[:, i, :], src, ACT.Square, accum_out=acc).then_inc(sq_done, 1)

            for c in range(C_OUT, C_END):
                chunk(c)
                squares(c)
            act.wait_ge(norm_step, 6 * QT + 2)
            A(root[:, :], var[:, :], ACT.Sqrt).then_inc(rooted, 1)
            act.wait_ge(norm_step, 6 * QT + 7)
            for i in range(1, QT, 2):
                act.wait_ge(hg_ready, 4 * QT)
                A(hres[:, i, :], hres[:, i, :], ACT.Copy, scale=rstd[:, i:i + 1]).then_inc(y_ready[1], 1)

        @block.vector
        def _(dve):
            V = nc.vector

            def split_lo(c, s):
                if isinstance(c, int) and NS * c + s >= NS * C_END:
                    return
                dve.wait_ge(strip_hi, c * NS + (s + 1))
                V.tensor_tensor(w_lo[:, s % RING, :, :], stage[:, s % 2, :, :],
                                w_hi[:, s % RING, :, :].bitcast(F), ALU.subtract).then_inc(strip_lo, 1)

            def chunk(c, steps=()):
                for s in range(NS):
                    split_lo(c, s + LEAD)
                    if s < len(steps) and steps[s]:
                        steps[s]()

            def rsqrt(cols, k, first):
                def step(ins):
                    ins.then_inc(norm_step, 1)
                v_, r_, t_, y_, s_ = (t[:, cols] for t in (var, root, tmp, rinv, ss))
                step(V.tensor_scalar(v_, s_, 1.0 / D_MODEL, EPS, ALU.mult, ALU.add))
                dve.wait_ge(rooted, k)
                step(V.reciprocal(y_, r_))
                dve.wait_ge(norm_step, first + 2)
                step(V.tensor_tensor(t_, y_, y_, ALU.mult))
                dve.wait_ge(norm_step, first + 3)
                step(V.tensor_tensor(t_, t_, v_, ALU.mult))
                dve.wait_ge(norm_step, first + 4)
                step(V.tensor_scalar(t_, t_, -0.5, 1.5, ALU.mult, ALU.add))
                dve.wait_ge(norm_step, first + 5)
                step(V.tensor_tensor(rstd[:, cols], y_, t_, ALU.mult))

            for h in range(HEADS):
                V.memset(slope[:, h:h + 1], -(2.0 ** (-8.0 * (h + 1) / HEADS)))
            dve.wait_ge(masks, 3)
            V.tensor_scalar(big_ident[:, :], ident[:, :], BIG, None, ALU.mult)
            V.tensor_copy(neg_tri[:, :], cst[:, 0, :])
            V.tensor_copy(neg_one[:, :], cst[:, 1, :]).then_inc(consts, 1)

            def turned_u_low(i):
                for j in range(4):
                    dve.wait_ge(u_hi_ready, 4 * i + j + 1)
                    V.tensor_tensor(u_lo[:, 4 * j:4 * j + 4, P * i:P * i + P],
                                    attn[j][:, :].rearrange("p (t s) -> p t s", t=4),
                                    u_hi[:, 4 * j:4 * j + 4, P * i:P * i + P].bitcast(F),
                                    ALU.subtract).then_inc(u_lo_ready, 1)

            for i in range(QT):
                dve.wait_ge(sumsq, i + 1)
                rsqrt(slice(i, i + 1), i + 1, 6 * i)
                dve.wait_ge(norm_step, 6 * i + 6)
                dve.wait_ge(xg_ready, i + 1)
                V.tensor_scalar(xg[:, i, :], xg[:, i, :], rstd[:, i:i + 1], None, ALU.mult).then_inc(xn_ready, 1)
                if i:
                    turned_u_low(i - 1)
            dve.wait_ge(ixw_hi_ready, 1)
            V.tensor_tensor(ixw_lo[:, :, :], ixw[:, :, :], ixw_hi[:, :, :].bitcast(F),
                            ALU.subtract).then_inc(ixw_lo_ready, 1)
            turned_u_low(QT - 1)
            for s in range(LEAD):
                split_lo(0, s)
            dve.wait_ge(kix_hi_ready, 1)
            dve.wait_ge(kw_copied, 1)
            V.tensor_tensor(kix_lo[0:IDX_DIM, :], proj[3][0:IDX_DIM, :], kix_hi[0:IDX_DIM, :].bitcast(F),
                            ALU.subtract).then_inc(kix_lo_ready, 1)
            dve.wait_ge(far_ready, 1)
            V.memset(far[0:P // 2, P // 2:P], BIG)
            dve.wait_ge(wix_turned, 1)
            V.tensor_scalar(wix[:, :, :],
                            attn[0][:, 0:QT * KW].rearrange("p (i e) -> p i e", i=QT)[:, :, IDX_DIM:KW],
                            IDX_HEADS ** -0.5 * IDX_DIM ** -0.5, None, ALU.mult).then_inc(wix_ready, 1)

            for c in range(C_QIX, C_SB):
                chunk(c)
                for e in range(4):
                    dve.wait_ge(qix_hi_ready, 4 * c + e + 1)
                    V.tensor_tensor(area_r[:, 24 + 4 * c + e, :], proj[e][:, :],
                                    area_r[:, 16 + 4 * c + e, :].bitcast(F), ALU.subtract).then_inc(proj_free, 1)

            def score_step(qi, s):
                w = WQ[qi]
                acc = score[:, qi % 2, 0:w]
                for h in (2 * s, 2 * s + 1):
                    n = IDX_HEADS * (qi - 1) + h
                    dve.wait_ge(relu_ready, n + 1)
                    if h == 0:
                        if n == 0:
                            dve.wait_ge(wix_ready, 1)
                        V.tensor_scalar(acc, relu[:, n % 2, 0:w], wix[:, qi, h:h + 1], None,
                                        ALU.mult).then_inc(relu_used, 1)
                    else:
                        dve.wait_ge(relu_used, n)
                        V.scalar_tensor_tensor(acc, relu[:, n % 2, 0:w], wix[:, qi, h:h + 1], acc,
                                               ALU.mult, ALU.add).then_inc(relu_used, 1)
                if s == NS - 1:
                    dve.wait_ge(relu_used, IDX_HEADS * qi)
                    V.memset(score[0:P // 2, qi % 2, w - P // 2:w], HIDDEN).then_inc(pick_step, 1)

            ROUNDS = TOPK // 8
            PICK = 2 * ROUNDS + 2

            def pick_round(qi, r):
                w = WQ[qi]
                acc = score[:, qi % 2, 0:w]
                base = PICK * (qi - 1) + 2 * r + 1
                dve.wait_ge(pick_step, base)
                V.max(top8[:, :], acc).then_inc(pick_step, 1)
                dve.wait_ge(pick_step, base + 1)
                V.match_replace(acc, top8[:, :], acc, TAKEN).then_inc(pick_step, 1)
                if r == ROUNDS - 1:
                    dve.wait_ge(pick_step, base + 2)
                    V.tensor_scalar(acc, acc, TAKEN, BIG, ALU.not_equal, ALU.mult).then_inc(pick_step, 1)
                    dve.wait_ge(pick_step, base + 3)
                    t = far[:, OQ[qi]:OQ[qi] + w]
                    V.tensor_tensor(t, t, acc, ALU.add).then_inc(far_ready, 1)

            for c in range(C_SB, C_SB + 4):
                qi = c - C_SB + 1

                def step(s, qi=qi):
                    def f():
                        if qi >= 2:
                            for r in range(ROUNDS // NS):
                                pick_round(qi - 1, ROUNDS // NS * s + r)
                        if qi < QT:
                            score_step(qi, s)
                    return f

                chunk(c, [step(s) for s in range(NS)])
            with dve.Fori(C_SB + 4, C_SA) as c:
                chunk(c)

            def qk_low(hh, q_slot, k_slot):
                def f():
                    dve.wait_ge(qk_hi, hh * 2 + 2)
                    V.scalar_tensor_tensor(ql[:, :], area[:, ds(q_slot, 1), :], SCALE, qh[:, :].bitcast(F),
                                           ALU.mult, ALU.subtract).then_inc(qk_lo, 1)
                    V.tensor_tensor(kl[:, :], area[:, ds(k_slot, 1), :], kh[:, :].bitcast(F),
                                    ALU.subtract).then_inc(qk_lo, 1)
                return f

            def v_low(hh):
                dve.wait_ge(v_hi, hh + 1)
                V.tensor_tensor(vl[:, :], attn[3][:, :], vh[:, :].bitcast(F), ALU.subtract).then_inc(v_lo, 1)

            def silu(hh, z_slot):
                dve.wait_ge(gate_exp, hh + 1)
                V.tensor_scalar(og[:, :], og[:, :], 1.0, None, ALU.add).then_inc(silu_step, 1)
                dve.wait_ge(silu_step, hh * 3 + 1)
                V.reciprocal(og[:, :], og[:, :]).then_inc(silu_step, 1)
                dve.wait_ge(silu_step, hh * 3 + 2)
                V.tensor_tensor(og[:, :], og[:, :], area[:, ds(z_slot, 1), :], ALU.mult).then_inc(silu_step, 1)

            def gated(hh):
                dve.wait_ge(av_done, hh + 1)
                dve.wait_ge(silu_step, hh * 3 + 3)
                V.tensor_tensor(og[:, :], attn[0][:, :], og[:, :], ALU.mult).then_inc(o_ready, 1)

            def sb_steps(n):
                def softplus(i):
                    w = WK[i]
                    dve.wait_ge(e_ready, n * 4 + i + 1)
                    if i >= 2:
                        dve.wait_ge(sp_lo, n * 4 + i - 1)
                    V.scalar_tensor_tensor(full[:, i % 2, 0:w], attn[i][:, 0:w], 0.0, eb[:, i % 2, 0:w],
                                           ALU.max, ALU.add).then_inc(sp_step, 1)
                    dve.wait_ge(sp_step, n * 4 + i + 1)
                    t = full[:, i % 2, 0:P]
                    V.tensor_tensor(t, t, before[:, :], ALU.mult).then_inc(sp_ready, 1)

                def sp_low(i):
                    w = WK[i]
                    dve.wait_ge(sp_hi, n * 4 + i + 1)
                    V.tensor_tensor(x_lo[:, OK[i]:OK[i] + w], full[:, i % 2, 0:w],
                                    x_hi[:, OK[i]:OK[i] + w].bitcast(F), ALU.subtract).then_inc(sp_lo, 1)

                def weights_low(i):
                    w = WK[i]
                    dve.wait_ge(w_full, n * 8 + 2 * i + 2)
                    V.tensor_tensor(x_lo[:, OK[i]:OK[i] + w], full[:, i % 2, 0:w],
                                    x_hi[:, OK[i]:OK[i] + w].bitcast(F), ALU.subtract).then_inc(w_low, 1)

                def s1():
                    v_low(n)
                    softplus(0)
                    softplus(1)

                def s2():
                    sp_low(0)
                    softplus(2)
                    sp_low(1)

                def s3():
                    softplus(3)
                    sp_low(2)
                    sp_low(3)

                def s5():
                    weights_low(0)
                    weights_low(1)

                def s6():
                    weights_low(2)
                    weights_low(3)

                return [qk_low(n, n, n + HEADS), s1, s2, s3,
                        lambda: silu(n, n + 3 * HEADS), s5, s6, lambda: gated(n)]

            with dve.Fori(0, HEADS) as n:
                chunk(n + C_SA, sb_steps(n))

            def sa_steps(n, slot):
                hh = n + HEADS

                def logits(i):
                    w = WQ[i]
                    t = p_sa[:, OQ[i]:OQ[i] + w]
                    dve.wait_ge(z_done, hh * 4 + i + 1)
                    V.scalar_tensor_tensor(t, far[:, OQ[i]:OQ[i] + w], slope[:, ds(n, 1)], attn[i][:, 0:w],
                                           ALU.mult, ALU.add).then_inc(lg_ready, 1)
                    dve.wait_ge(lg_ready, n * 4 + i + 1)
                    V.tensor_reduce(nmax[:, i:i + 1], t, AX.X, ALU.max, negate=True).then_inc(max_ready, 1)

                def normalize(i):
                    dve.wait_ge(p_exp, n * 4 + i + 1)
                    V.reciprocal(pinv[:, i:i + 1], psum_p[:, i:i + 1]).then_inc(inv_ready, 1)
                    dve.wait_ge(inv_ready, n * 4 + i + 1)
                    t = p_sa[:, OQ[i]:OQ[i] + WQ[i]]
                    V.tensor_scalar(t, t, pinv[:, i:i + 1], None, ALU.mult).then_inc(p_ready, 1)

                def turned_low(i):
                    dve.wait_ge(pt_hi, n * 4 + i + 1)
                    V.tensor_tensor(x_lo[:, OK[i]:OK[i] + WK[i]], attn[i][:, 0:WK[i]],
                                    x_hi[:, OK[i]:OK[i] + WK[i]].bitcast(F), ALU.subtract).then_inc(w_low, 1)

                def s1():
                    v_low(hh)
                    logits(0)
                    logits(1)

                def s2():
                    logits(2)
                    logits(3)

                def s3():
                    normalize(0)
                    normalize(1)

                def s4():
                    normalize(2)
                    normalize(3)
                    silu(hh, slot(3))

                def s5():
                    for i in range(QT):
                        turned_low(i)

                return [qk_low(hh, slot(0), slot(1)), s1, s2, s3, s4, s5, None, lambda: gated(hh)]

            dve.wait_ge(far_ready, QT)
            with dve.Fori(0, 2) as a:
                with dve.Fori(0, 4) as b:
                    n = a * 4 + b
                    chunk(n + C_GATE, sa_steps(n, lambda kind: b * 8 + a + 2 * kind))

            def o_low(ts):
                def f():
                    for t in ts:
                        dve.wait_ge(o_hi, t + 1)
                        V.tensor_tensor(u_lo[:, t, :], o_in[:, t % HEADS, :], u_hi[:, t, :].bitcast(F),
                                        ALU.subtract).then_inc(o_lo, 1)
                return f

            def slot_of(c, e, lo):
                if isinstance(c, int):
                    return slice(8 * (c - C_BRANCH) + 2 * e + lo, 8 * (c - C_BRANCH) + 2 * e + lo + 1)
                return ds(c * 8 + (2 * e + lo - 8 * C_BRANCH), 1)

            def mix_sb(c):
                m = c - C_BRANCH

                def f():
                    for e in range(4):
                        bank_done(dve, c, e, strips=NS // 2)
                        dve.wait_ge(sigmoid_ready, m * 4 + e + 1)
                        V.tensor_tensor(mix[:, e, :], proj[e][:, :], area[:, slot_of(c, e, 0), :],
                                        ALU.mult).then_inc(proj_free, 1)
                return f

            def mix_both(c):
                m = c - C_BRANCH
                for e in range(4):
                    bank_done(dve, c, e, done=branch_sa_done, m=m)
                    if not (isinstance(c, int) and e == 0):
                        dve.wait_ge(mix_ready, m * 4 + e)
                    V.tensor_tensor(mix_sa[:, :], attn[e][:, :], area[:, slot_of(c, e, 1), :],
                                    ALU.mult).then_inc(attn_free, 1)
                    dve.wait_ge(attn_free, m * 4 + e + 1)
                    if e == 0:
                        dve.wait_ge(proj_free, c * 4 + 4)
                    V.tensor_tensor(mix[:, e, :], mix[:, e, :], mix_sa[:, :], ALU.add).then_inc(mix_ready, 1)
                for e in range(4):
                    dve.wait_ge(mix_hi, m * 4 + e + 1)
                    V.tensor_tensor(area_r[:, slot_of(c, e, 1), :], mix[:, e, :],
                                    area_r[:, slot_of(c, e, 0), :].bitcast(F), ALU.subtract).then_inc(mix_lo, 1)

            o_low(range(0, 8))()
            chunk(C_BRANCH, [o_low(range(8, 12)), o_low(range(12, 16)), None, None, None, mix_sb(C_BRANCH)])
            mix_both(C_BRANCH)
            with dve.Fori(C_BRANCH + 1, C_OUT) as c:
                chunk(c, [None, None, None, None, None, mix_sb(c)])
                mix_both(c)

            def residual(c):
                m = c - C_OUT
                sl = slice(CW * m, CW * m + CW) if isinstance(c, int) else ds(m * CW, CW)
                for i in range(QT):
                    t = hres[:, i, sl]
                    bank_done(dve, c, i)
                    V.tensor_tensor(t, proj[i][:, :], t, ALU.add).then_inc(h_ready, 1)
                for i in range(QT):
                    t = hres[:, i, sl]
                    dve.wait_ge(sq_done, m * 4 + i + 1)
                    V.tensor_tensor(t, t, fgain[:, sl], ALU.mult).then_inc(hg_ready, 1)

            for c in range(C_OUT, C_END):
                chunk(c)
                if c == C_OUT:
                    dve.wait_ge(res_loaded, 16)
                    dve.wait_ge(fgain_loaded, 16)
                residual(c)
            V.tensor_reduce(ss[:, :], ssq[:, :, :], AX.X, ALU.add).then_inc(norm_step, 1)
            dve.wait_ge(norm_step, 6 * QT + 1)
            rsqrt(slice(0, QT), QT + 1, 6 * QT + 1)
            dve.wait_ge(norm_step, 6 * QT + 7)
            dve.wait_ge(hg_ready, 4 * QT)
            for i in range(0, QT, 2):
                V.tensor_scalar(hres[:, i, :], hres[:, i, :], rstd[:, i:i + 1], None, ALU.mult
                                ).then_inc(y_ready[0], 1)

        @block.tensor
        def _(pe):
            def mm3(out_, a_hi, a_lo, b_hi, b_lo, start, stop, free=False):
                nc.tensor.matmul(out_, a_hi, b_hi, start=start, stop=False, skip_group_check=free)
                nc.tensor.matmul(out_, a_hi, b_lo, start=False, stop=False, skip_group_check=free)
                return nc.tensor.matmul(out_, a_lo, b_hi, start=False, stop=stop, skip_group_check=free)

            def strip(c, s, first, last, tokens=False, banks=proj, free_of=None, done=proj_done):
                pe.wait_ge(strip_lo, c * NS + (s + 1))
                for j in range(2):
                    t = 2 * s + j
                    for e in range(4):
                        st, en = first and j == 0, last and j == 1
                        if st and free_of is not None:
                            free_of(e)
                        cols = slice(P * e, P * e + P)
                        r = s % RING
                        if tokens:
                            m = mm3(banks[e][:, :], area_r[:, 2 * t, cols], area_r[:, 2 * t + 1, cols],
                                    w_hi[:, r, j, :], w_lo[:, r, j, :], st, en)
                        else:
                            m = mm3(banks[e][:, :], w_hi[:, r, j, cols], w_lo[:, r, j, cols],
                                    u_hi[:, t, :], u_lo[:, t, :], st, en)
                        if en and e < 3:
                            m.then_inc(done, 1)
                m.then_inc(strip_used, 1)

            def chunk(c, steps=(), tokens=False, ready=None):
                def bank_free(e):
                    if tokens and not isinstance(c, int):
                        pe.wait_ge(h_ready, c * 4 + (e - 3 - 4 * C_OUT))
                    elif not (isinstance(c, int) and c == 0):
                        pe.wait_ge(proj_free, c * 4 + (e - 3))
                    elif e == 3:
                        pe.wait_ge(kix_lo_ready, 1)
                for s in range(NS):
                    if ready:
                        ready(s)
                    strip(c, s, s == 0, s == NS - 1, tokens, free_of=bank_free)
                    if s < len(steps) and steps[s]:
                        steps[s]()

            pe.wait_ge(masks, 1)
            for i in range(QT):
                pe.wait_ge(xn_ready, i + 1)
                for j in range(4):
                    if i > 0:
                        pe.wait_ge(u_lo_ready, 4 * (i - 1) + j + 1)
                    for t in range(4):
                        k = 4 * j + t
                        m = nc.tensor.transpose(attn[j][:, P * t:P * t + P], xg[:, i, P * k:P * k + P], ident[:, :])
                    m.then_inc(xt_done, 1)
            pe.wait_ge(ixw_lo_ready, 1)
            for t in range(KT):
                if t % 4 == 0:
                    pe.wait_ge(u_lo_ready, 4 * (QT - 1) + t // 4 + 1)
                m = mm3(proj[3][0:KW, :], ixw_hi[:, t, :], ixw_lo[:, t, :], u_hi[:, t, :], u_lo[:, t, :],
                        t == 0, t == KT - 1)
            m.then_inc(kw_done, 1)

            def turn_wix():
                pe.wait_ge(kw_copied, 1)
                for i in range(QT):
                    m = nc.tensor.transpose(attn[0][:, KW * i:KW * i + KW], kw_t[0:KW, P * i:P * i + P],
                                            ident[0:KW, 0:KW])
                m.then_inc(wix_turned, 1)

            chunk(C_QIX, [turn_wix])
            for c in range(C_QIX + 1, C_SB):
                chunk(c)

            def dots(qi, s):
                def f():
                    for h in (2 * s, 2 * s + 1):
                        n = IDX_HEADS * (qi - 1) + h
                        if n == 0:
                            pe.wait_ge(kix_both, 32)
                            pe.wait_ge(wix_ready, 1)
                            pe.wait_ge(proj_free, 4 * C_SB)
                        if n >= 4:
                            pe.wait_ge(relu_ready, n - 3)
                        b = IDX_DIM * (h % 2)
                        q = slice(P * qi, P * qi + P)
                        w = WQ[qi]
                        mm3(attn[h % 4][:, 0:w], area_r[b:b + IDX_DIM, 16 + h // 2, q],
                            area_r[b:b + IDX_DIM, 24 + h // 2, q],
                            kix_hi[b:b + IDX_DIM, 0:w], kix_lo[b:b + IDX_DIM, 0:w], True, True).then_inc(dots_done, 1)
                return f

            for c in range(C_SB, C_SB + 4):
                qi = c - C_SB + 1
                chunk(c, [dots(qi, s) for s in range(NS)] if qi < QT else ())
            with pe.Fori(C_SB + 4, C_SA) as c:
                chunk(c)

            def turn_v(hh):
                pe.wait_ge(v_staged, hh + 1)
                for i in range(QT):
                    m = nc.tensor.transpose(attn[3][:, P * i:P * i + P], v_t[:, P * i:P * i + P], ident[:, :])
                m.then_inc(v_turned, 1)

            def times_v(hh):
                pe.wait_ge(w_low, hh * 4 + 4)
                for i in range(QT):
                    k = slice(OK[i], OK[i] + WK[i])
                    v = slice(P * i, P * i + P)
                    m = mm3(attn[0][:, P * i:SEQ], vh[:, v], vl[:, v], x_hi[:, k], x_lo[:, k],
                            i == 0, i == QT - 1)
                m.then_inc(av_done, 1)

            def sb_steps(n):
                def z(i):
                    k = slice(P * i, P * i + P)
                    mm3(attn[i][:, 0:WK[i]], kh[:, k], kl[:, k], qh[:, P * i:SEQ], ql[:, P * i:SEQ],
                        True, True, True).then_inc(z_done, 1)

                def s0():
                    turn_v(n)
                    pe.wait_ge(qk_lo, n * 2 + 2)
                    for i in range(3):
                        z(i)

                def s1():
                    pe.wait_ge(v_lo, n + 1)
                    z(3)

                def s4():
                    pe.wait_ge(sp_lo, n * 4 + 4)
                    for i in range(QT):
                        for j in range(i, QT):
                            o_ = attn[i][:, P * (j - i):WK[i]]
                            a = neg_tri if i == j else neg_one
                            for part in (x_lo, x_hi):
                                nc.tensor.matmul(o_, a[:, :], part[:, OK[j]:OK[j] + WK[j]],
                                                 start=False, stop=False, skip_group_check=True)
                        nc.tensor.matmul(attn[i][:, 0:P], big_ident[:, :], neg_tri[:, :], start=False, stop=True,
                                         skip_group_check=True).then_inc(c_done, 1)

                return [s0, s1, None, None, s4, None, lambda: times_v(n)]

            pe.wait_ge(consts, 5)
            with pe.Fori(0, HEADS) as n:
                chunk(n + C_SA, sb_steps(n))

            def sa_steps(n):
                hh = n + HEADS

                def lg(i):
                    q = slice(P * i, P * i + P)
                    mm3(attn[i][:, 0:WQ[i]], qh[:, q], ql[:, q], kh[:, 0:WQ[i]], kl[:, 0:WQ[i]],
                        True, True).then_inc(z_done, 1)

                def s0():
                    turn_v(hh)
                    pe.wait_ge(qk_lo, hh * 2 + 2)
                    for i in range(3):
                        lg(i)

                def s1():
                    pe.wait_ge(v_lo, hh + 1)
                    lg(3)

                def s4():
                    pe.wait_ge(p_ready, n * 4 + 4)
                    for i in range(QT):
                        for q in range(i, QT):
                            m = nc.tensor.transpose(attn[i][:, P * (q - i):P * (q - i) + P],
                                                    p_sa[:, OQ[q] + P * i:OQ[q] + P * i + P], ident[:, :])
                        m.then_inc(pt_done, 1)

                return [s0, s1, None, None, s4, None, lambda: times_v(hh)]

            with pe.Fori(0, 2) as a:
                with pe.Fori(0, 4) as b:
                    n = a * 4 + b
                    chunk(n + C_GATE, sa_steps(n))

            def branch_chunk(c):
                m_ = c - C_BRANCH

                def sb_free(e):
                    pe.wait_ge(proj_free, c * 4 + (e - 3))

                def sa_free(e):
                    if isinstance(c, int):
                        pe.wait_ge(o_ready, 2 * HEADS)
                    else:
                        pe.wait_ge(attn_free, m_ * 4 + (e - 3))

                for s in range(NS):
                    if isinstance(c, int):
                        pe.wait_ge(o_lo, 2 * s + 2)
                    h = NS // 2
                    if s < h:
                        strip(c, s, s == 0, s == h - 1, free_of=sb_free)
                    else:
                        strip(c, s, s == h, s == NS - 1, banks=attn, free_of=sa_free, done=branch_sa_done)

            branch_chunk(C_BRANCH)
            with pe.Fori(C_BRANCH + 1, C_OUT) as c:
                branch_chunk(c)

            chunk(C_OUT, tokens=True, ready=lambda s: pe.wait_ge(mix_lo, 2 * s + 2))
            with pe.Fori(C_OUT + 1, C_END) as c:
                chunk(c, tokens=True)


_INS = ["x", "norm_gain", "w_in", "w_branch_sb", "w_branch_sa", "w_out", "final_norm_gain"]


def kernel(**inputs):
    import numpy as np
    import concourse.bacc as bacc
    from concourse.bass_utils import run_bass_kernel_spmd

    nc = bacc.Bacc("TRN2", target_bir_lowering=False, num_devices=1,
                   dynamic_dma_scratch_size=8192)
    arrays, args = {}, []
    for name in _INS:
        a = np.ascontiguousarray(inputs[name])
        arrays[f"in_{name}"] = a
        args.append(nc.dram_tensor(f"in_{name}", a.shape, mybir.dt.from_np(a.dtype), kind="ExternalInput").ap())
    args.append(nc.dram_tensor("out_h", (1, SEQ, D_MODEL), mybir.dt.float32, kind="ExternalOutput").ap())
    build(nc, *args)
    r = run_bass_kernel_spmd(nc, [arrays], core_ids=[0])
    return r.results[0]["out_h"]
```

```python
from contextlib import ExitStack

import concourse.bass as bass
from concourse import mybir

D_MODEL, SEQ = 2048, 512
HEADS, HD = 8, 128
IDX_HEADS, IDX_DIM = 16, 64
TOPK = min(256, SEQ // 4)
EPS = 1e-6
P = 128
QT = SEQ // P
KT = D_MODEL // P
CW = 512
NS = KT // 2
RING = 4
LEAD = 2
BIG = 1e30
HIDDEN, TAKEN = -3.0e38, -3.4e38

COL_SB = 0
COL_QIX = 8 * HEADS * HD
COL_KIX = COL_QIX + IDX_HEADS * IDX_DIM
KW = IDX_DIM + IDX_HEADS
COL_GATE = COL_KIX + KW

C_QIX, C_SB, C_SA, C_GATE, C_BRANCH, C_OUT, C_END = 0, 2, 10, 18, 26, 30, 34
C_LAST = C_END - 1
SHARED = 3

WK = [SEQ - P * i for i in range(QT)]
OK = [sum(WK[:i]) for i in range(QT)]
WQ = [P * (i + 1) for i in range(QT)]
OQ = [sum(WQ[:i]) for i in range(QT)]
TRI = sum(WK)
SMALL = 1024


def build(nc, x, norm_gain, w_in, w_branch_sb, w_branch_sa, w_out, final_gain, out):
    F, R, I = mybir.dt.float32, mybir.dt.float32r, mybir.dt.int32
    ALU, ACT, AX = mybir.AluOpType, mybir.ActivationFunctionType, mybir.AxisListType
    ds = bass.ds

    place = {}

    def at(name, shape, dt, offset):
        return nc.alloc_sbuf_tensor_at(name, [P] + shape, dt, offset=offset)

    top = [(nc.sbuf_base + 31) // 32 * 32]

    def region(name, size):
        place[name] = top[0]
        top[0] += size
        return place[name]

    TILE = 4 * SEQ
    region("u_hi", KT * TILE)
    region("u_lo", KT * TILE)
    region("area", 32 * TILE)
    region("stage", 2 * 2 * TILE)
    region("w_hi", RING * 2 * TILE)
    region("w_lo", RING * 2 * TILE)
    work = region("work", 11 * TILE + 2 * 4 * TRI)
    region("small", SMALL)
    region("far", 4 * TRI)
    region("const", 5 * 4 * P)
    region("v_t", TILE)
    region("spare", 3 * 1024)
    assert top[0] <= nc.sbuf_usable_end, top[0]

    u_hi = at("u_hi", [KT, SEQ], R, place["u_hi"])
    u_lo = at("u_lo", [KT, SEQ], R, place["u_lo"])
    hres = at("hres", [QT, D_MODEL], F, place["u_hi"])
    area = at("area", [32, SEQ], F, place["area"])
    area_r = at("area_r", [32, SEQ], R, place["area"])
    xs = at("xs", [QT, D_MODEL], F, place["area"])
    half = place["area"] + 16 * TILE
    ixw = at("ixw", [KT, KW], F, half)
    ixw_hi = at("ixw_hi", [KT, KW], R, half + 4 * KT * KW)
    ixw_lo = at("ixw_lo", [KT, KW], R, half + 8 * KT * KW)
    stage = at("stage", [2, 2, CW], F, place["stage"])
    w_hi = at("w_hi", [RING, 2, CW], R, place["w_hi"])
    w_lo = at("w_lo", [RING, 2, CW], R, place["w_lo"])

    qh, ql, kh, kl, vh, vl = [at(n, [SEQ], R, work + i * TILE)
                              for i, n in enumerate(["qh", "ql", "kh", "kl", "vh", "vl"])]
    x_hi = at("x_hi", [TRI], R, work + 6 * TILE)
    p_sa = at("p_sa", [TRI], F, work + 6 * TILE)
    x_lo = at("x_lo", [TRI], R, work + 6 * TILE + 4 * TRI)
    w2 = work + 6 * TILE + 8 * TRI
    full = at("full", [2, SEQ], F, w2)
    eb = at("eb", [2, SEQ], F, w2 + 2 * TILE)
    v_t = at("v_t", [SEQ], F, place["v_t"])
    og = at("og", [SEQ], F, w2 + 4 * TILE)
    gain = at("gain", [D_MODEL], F, work)
    junk = at("junk", [D_MODEL], F, work + 4 * TILE)
    xg = at("xg", [QT, D_MODEL], F, place["w_hi"])
    kix_hi = at("kix_hi", [SEQ], R, work)
    kix_lo = at("kix_lo", [SEQ], R, work + TILE)
    kw_t = at("kw_t", [SEQ], F, work + 2 * TILE)
    relu = at("relu", [2, SEQ], F, work + 8 * TILE)
    score = at("score", [2, SEQ], F, work + 10 * TILE)
    dist_i = at("dist_i", [TRI], I, work + 3 * TILE)
    o_first = at("o_first", [4, SEQ], F, w2)
    o_in = at("o_in", [8, SEQ], F, work)
    mix = at("mix", [QT, SEQ], F, work + 8 * TILE)
    mix_sa = at("mix_sa", [SEQ], F, work + 12 * TILE)
    fgain = at("fgain", [D_MODEL], F, place["far"])
    junk2 = at("junk2", [2, CW], F, place["far"] + 4 * D_MODEL)
    assert place["far"] + 4 * D_MODEL + 8 * CW <= top[0]
    last_hi = at("last_hi", [KT - 2 * SHARED, CW], R, place["u_lo"])
    last_lo = at("last_lo", [KT - 2 * SHARED, CW], R, work)

    far = at("far", [TRI], F, place["far"])
    ident = at("ident", [P], F, place["const"])
    big_ident = at("big_ident", [P], R, place["const"] + 4 * P)
    neg_tri = at("neg_tri", [P], R, place["const"] + 8 * P)
    neg_one = at("neg_one", [P], R, place["const"] + 12 * P)
    before = at("before", [P], F, place["const"] + 16 * P)
    cst = at("cst", [2, P], F, w2 + 4 * TILE)

    small_at = [place["small"]]

    def small(name, shape):
        size = 4
        for d in shape:
            size *= d
        small_at[0] += (size + 31) // 32 * 32
        assert small_at[0] <= place["small"] + SMALL
        return at(name, shape, F, small_at[0] - (size + 31) // 32 * 32)

    wix = small("wix", [QT, IDX_HEADS])
    top8 = small("top8", [8])
    ss, var, root, rinv, tmp, rstd = [small(n, [QT]) for n in ("ss", "var", "root", "rinv", "tmp", "rstd")]
    nmax, psum_p, pinv = [small(n, [QT]) for n in ("nmax", "psum_p", "pinv")]
    slope = small("slope", [HEADS])
    ssq = small("ssq", [QT, 4])

    proj = [nc.alloc_psum_tensor(f"proj{i}", [P, CW], F) for i in range(4)]
    attn = [nc.alloc_psum_tensor(f"attn{i}", [P, CW], F) for i in range(4)]

    o_dram = nc.dram_tensor("o_scratch", (2 * HEADS, P, SEQ), F, kind="Internal").ap()

    win = w_in[0].rearrange("(t p) e -> p t e", p=P)
    wsb = w_branch_sb[0].rearrange("(t p) e -> p t e", p=P)
    wsa = w_branch_sa[0].rearrange("(t p) e -> p t e", p=P)
    wout = w_out[0].rearrange("(t p) e -> p t e", p=P)
    x_rows = x[0].rearrange("(i p) d -> i p d", p=P)
    out_rows = out[0].rearrange("(i p) d -> i p d", p=P)

    def sem(name):
        return nc.alloc_semaphore(name)

    strip_loaded = [sem("strip_loaded0"), sem("strip_loaded1")]
    strip_hi, strip_lo, strip_used = sem("strip_hi"), sem("strip_lo"), sem("strip_used")
    proj_done, proj_free = sem("proj_done"), sem("proj_free")
    x_loaded = [sem(f"x_loaded{i}") for i in range(QT)]
    gain_loaded, ixw_loaded, consts, masks = sem("gain_loaded"), sem("ixw_loaded"), sem("consts"), sem("masks")
    xg_ready, sumsq, norm_step, rooted, xn_ready = sem("xg_ready"), sem("sumsq"), sem("norm_step"), sem("rooted"), sem("xn_ready")
    xt_done, u_hi_ready, u_lo_ready = sem("xt_done"), sem("u_hi_ready"), sem("u_lo_ready")
    ixw_hi_ready, ixw_lo_ready, kw_done, kw_copied = sem("ixw_hi_ready"), sem("ixw_lo_ready"), sem("kw_done"), sem("kw_copied")
    kix_hi_ready, kix_lo_ready = sem("kix_hi_ready"), sem("kix_lo_ready")
    wix_turned, wix_ready, dist_ready, far_ready = sem("wix_turned"), sem("wix_ready"), sem("dist_ready"), sem("far_ready")
    qix_hi_ready = sem("qix_hi_ready")
    dots_done, relu_ready, relu_used, pick_step = sem("dots_done"), sem("relu_ready"), sem("relu_used"), sem("pick_step")
    v_staged, qk_hi, qk_lo = sem("v_staged"), sem("qk_hi"), sem("qk_lo")
    v_turned, v_hi, v_lo = sem("v_turned"), sem("v_hi"), sem("v_lo")
    z_done, e_step, e_ready, sp_step, sp_ready = sem("z_done"), sem("e_step"), sem("e_ready"), sem("sp_step"), sem("sp_ready")
    sp_hi, sp_lo, c_done = sem("sp_hi"), sem("sp_lo"), sem("c_done")
    w_full, w_low, av_done = sem("w_full"), sem("w_low"), sem("av_done")
    gate_exp, silu_step, o_ready, o_stored = sem("gate_exp"), sem("silu_step"), sem("o_ready"), sem("o_stored")
    lg_ready, max_ready, p_exp, inv_ready, p_ready = sem("lg_ready"), sem("max_ready"), sem("p_exp"), sem("inv_ready"), sem("p_ready")
    pt_done, pt_hi = sem("pt_done"), sem("pt_hi")
    sigmoid_ready = sem("sigmoid_ready")
    o_loaded = [sem(f"o_loaded{i}") for i in range(4)]
    o_hi, o_lo = sem("o_hi"), sem("o_lo")
    branch_sa_done, attn_free, mix_step, mix_ready, mix_hi, mix_lo = (
        sem("branch_sa_done"), sem("attn_free"), sem("mix_step"), sem("mix_ready"), sem("mix_hi"), sem("mix_lo"))
    res_loaded, fgain_loaded, h_ready, sq_done, y_stored = (
        sem("res_loaded"), sem("fgain_loaded"), sem("h_ready"), sem("sq_done"), sem("y_stored"))
    y_ready = [sem("y_ready_v"), sem("y_ready_s")]
    YV = 1280
    hg_ready, last_done = sem("hg_ready"), sem("last_done")

    SCALE = float(HD) ** -0.5
    HALVES = (slice(0, IDX_DIM), slice(IDX_DIM, P))

    def returned(t):
        return o_first[:, t, :] if t < 4 else o_in[:, (t - 4) % 8, :]

    def bank_done(eng, c, e, strips=NS, done=proj_done, m=None):
        if e < 3:
            eng.wait_ge(done, (c if m is None else m) * 3 + (e + 1))
        else:
            eng.wait_ge(strip_used, c * NS + strips)

    block = nc.Block()

    with block:
        @block.sync
        def _(sp):
            for i in range(QT):
                sp.dma_start(xs[:, i, :], x_rows[i]).then_inc(x_loaded[i], 16)
                if i == 0:
                    sp.dma_start(gain[:, :], norm_gain[0:1, :].to_broadcast([P, D_MODEL])
                                 ).then_inc(gain_loaded, 16)
            sp.dma_start(ixw[:, :, :], win[:, :, COL_KIX:COL_KIX + KW]).then_inc(ixw_loaded, 16)

            def load_strip(c, s, src):
                if not (isinstance(c, int) and NS * c + s < 2):
                    sp.wait_ge(strip_lo, c * NS + (s - 1))
                sp.dma_start(stage[:, s % 2, :, :], src).then_inc(strip_loaded[s % 2], 16)

            def load_chunk(c, source, col):
                for s in range(NS):
                    load_strip(c, s, source(s)[:, :, ds(col, CW)] if not isinstance(col, int)
                               else source(s)[:, :, col:col + CW])

            def rows(w):
                return lambda s: w[:, 2 * s:2 * s + 2, :]

            def branch_rows(s):
                return (wsb if s < NS // 2 else wsa)[:, 2 * (s % (NS // 2)):2 * (s % (NS // 2)) + 2, :]

            for c in range(C_QIX, C_SB):
                load_chunk(c, rows(win), COL_QIX + CW * c)
            with sp.Fori(C_SB, C_GATE) as c:
                load_chunk(c, rows(win), c * CW - C_SB * CW)
            with sp.Fori(C_GATE, C_BRANCH) as c:
                load_chunk(c, rows(win), c * CW + (COL_GATE - C_GATE * CW))
            with sp.Fori(C_BRANCH, C_OUT) as c:
                load_chunk(c, branch_rows, c * CW - C_BRANCH * CW)
            with sp.Fori(C_OUT, C_END) as c:
                load_chunk(c, rows(wout), c * CW - C_OUT * CW)
            for i in range(QT):
                for part, cols in enumerate((slice(0, YV), slice(YV, D_MODEL))):
                    sp.wait_ge(y_ready[part], i + 1)
                    sp.dma_start(out_rows[i][:, cols], hres[:, i, cols]).then_inc(y_stored, 16)
            sp.wait_ge(y_stored, 16 * 2 * QT)

        @block.gpsimd
        def _(pool):
            g = nc.gpsimd
            g.memset(ident[:, :], 0.0).then_inc(consts, 1)
            g.memset(before[:, :], 1.0).then_inc(consts, 1)
            g.memset(cst[:, 0, :], 0.0).then_inc(consts, 1)
            g.memset(cst[:, 1, :], -1.0).then_inc(consts, 1)
            pool.wait_ge(consts, 4)
            g.affine_select(out=ident[:, :], in_=ident[:, :], compare_op=ALU.not_equal, fill=1.0,
                            base=0, pattern=[[-1, P]], channel_multiplier=1).then_inc(masks, 1)
            g.affine_select(out=before[:, :], in_=before[:, :], compare_op=ALU.is_gt, fill=0.0,
                            base=0, pattern=[[1, P]], channel_multiplier=-1).then_inc(masks, 1)
            g.affine_select(out=cst[:, 0, :], in_=cst[:, 0, :], compare_op=ALU.is_gt, fill=-1.0,
                            base=0, pattern=[[1, P]], channel_multiplier=-1).then_inc(masks, 1)
            pool.wait_ge(gain_loaded, 16)
            for i in range(2, QT):
                pool.wait_ge(x_loaded[i], 16)
                g.tensor_tensor(xg[:, i, :], xs[:, i, :], gain[:, :], ALU.mult).then_inc(xg_ready, 1)
            pool.wait_ge(sumsq, QT)
            pool.wait_ge(xn_ready, QT)
            for i in range(QT):
                g.iota(dist_i[:, OQ[i]:OQ[i] + WQ[i]], pattern=[[-1, WQ[i]]], base=P * i,
                       channel_multiplier=1).then_inc(dist_ready, 1)

            def head(hh, v_slot, store):
                g.tensor_copy(v_t[:, :], area[:, ds(v_slot, 1), :]).then_inc(v_staged, 1)
                pool.wait_ge(o_ready, hh + 1)
                pool.dma_start(store, og[:, :]).then_inc(o_stored, 16)
                pool.wait_ge(o_stored, hh * 16 + 16)

            pool.wait_ge(proj_free, 4 * C_SA)
            pool.wait_ge(far_ready, QT)
            with pool.Fori(0, HEADS) as n:
                head(n, n + 2 * HEADS, o_dram[ds(n, 1)].rearrange("a p s -> p (a s)"))
            def outputs_back(j):
                dst = o_first[:, :, :] if j == 0 else o_in[:, 4 * ((j - 1) % 2):4 * ((j - 1) % 2) + 4, :]
                pool.dma_start(dst, o_dram[4 * j:4 * j + 4].rearrange("a p s -> p a s")).then_inc(o_loaded[j], 16)

            outputs_back(0)
            pool.wait_ge(proj_free, 4 * C_GATE)
            with pool.Fori(0, 2) as a:
                with pool.Fori(0, 4) as b:
                    n = a * 4 + b
                    head(n + HEADS, b * 8 + a + 4, o_dram[ds(n + HEADS, 1)].rearrange("a p s -> p (a s)"))

            pool.wait_ge(av_done, 2 * HEADS)
            outputs_back(1)
            outputs_back(2)
            pool.wait_ge(o_lo, 8)
            outputs_back(3)
            pool.wait_ge(strip_used, NS * C_OUT)
            pool.dma_start(hres[:, :, :], x[0].rearrange("(i p) d -> p i d", p=P)).then_inc(res_loaded, 16)
            pool.dma_start(fgain[:, :], final_gain.rearrange("(a d) -> a d", a=1).to_broadcast([P, D_MODEL])
                           ).then_inc(fgain_loaded, 16)

        @block.scalar
        def _(act):
            A = nc.scalar.activation

            def split_hi(c, s):
                act.wait_ge(strip_loaded[s % 2], c * (16 * NS // 2) + 16 * (s // 2 + 1))
                if not (isinstance(c, int) and NS * c + s < RING):
                    act.wait_ge(strip_used, c * NS + (s - RING + 1))
                A(w_hi[:, s % RING, :, :], stage[:, s % 2, :, :], ACT.Copy).then_inc(strip_hi, 1)

            def chunk(c, steps=()):
                for s in range(NS):
                    split_hi(c, s + LEAD)
                    if s < len(steps) and steps[s]:
                        steps[s]()

            def apart():
                act.nop(nofuse=True)

            def evacuate(c, dst):
                for e in range(4):
                    bank_done(act, c, e)
                    apart()
                    A(dst(e), proj[e][:, :], ACT.Copy).then_inc(proj_free, 1)

            def turned_u_high(i):
                for j in range(4):
                    act.wait_ge(xt_done, 4 * i + j + 1)
                    A(u_hi[:, 4 * j:4 * j + 4, P * i:P * i + P],
                      attn[j][:, :].rearrange("p (t s) -> p t s", t=4), ACT.Copy).then_inc(u_hi_ready, 1)

            nc.scalar.preload_act_table_set("sqrt_and_others")
            for i in range(QT):
                act.wait_ge(x_loaded[i], 16)
                if i:
                    act.wait_ge(sumsq, i)
                A(junk[:, :], xs[:, i, :], ACT.Square, accum_out=ss[:, i:i + 1]).then_inc(sumsq, 1)
                act.wait_ge(norm_step, 6 * i + 1)
                A(root[:, i:i + 1], var[:, i:i + 1], ACT.Sqrt).then_inc(rooted, 1)
                if i == QT - 1:
                    act.wait_ge(ixw_loaded, 16)
                    A(ixw_hi[:, :, :], ixw[:, :, :], ACT.Copy).then_inc(ixw_hi_ready, 1)
                if i:
                    turned_u_high(i - 1)
            turned_u_high(QT - 1)
            act.wait_ge(xt_done, 4 * QT)
            for s in range(LEAD):
                split_hi(0, s)
            act.wait_ge(kw_done, 1)
            for rows_ in HALVES:
                A(kix_hi[rows_, :], proj[3][0:IDX_DIM, :], ACT.Copy).then_inc(kix_hi_ready, 1)
            A(kw_t[0:KW, :], proj[3][0:KW, :], ACT.Copy).then_inc(kw_copied, 1)
            act.wait_ge(dist_ready, QT)
            A(far[:, :], dist_i[:, :], ACT.Abs).then_inc(far_ready, 1)

            nc.scalar.preload_act_table_set("natural_log_exp_and_others")
            for c in range(C_QIX, C_SB):
                chunk(c)
                for e in range(4):
                    bank_done(act, c, e)
                    for par, rows_ in enumerate(HALVES):
                        A(area_r[rows_, 16 + 8 * c + 2 * e + par, :], proj[e][rows_, :],
                          ACT.Copy).then_inc(qix_hi_ready, 1)

            def relu_step(qi, s):
                def f():
                    for h in (2 * s, 2 * s + 1):
                        n = IDX_HEADS * (qi - 1) + h
                        act.wait_ge(dots_done, n + 1)
                        if n >= 2:
                            act.wait_ge(relu_used, n - 1)
                        A(relu[:, n % 2, 0:WQ[qi]], attn[h % 4][:, 0:WQ[qi]], ACT.Relu).then_inc(relu_ready, 1)
                return f

            for c in range(C_SB, C_SB + 4):
                qi = c - C_SB + 1
                chunk(c, [relu_step(qi, s) for s in range(NS - 1)] if qi < QT else ())
                evacuate(c, lambda e: area[:, 4 * (c - C_SB) + e, :])
                if qi < QT:
                    relu_step(qi, NS - 1)()
            with act.Fori(C_SB + 4, C_SA) as c:
                chunk(c)
                evacuate(c, lambda e: area[:, ds(c * 4 + (e - 4 * C_SB), 1), :])

            def stage_qk(hh, q_slot, k_slot):
                def f():
                    act.wait_ge(strip_used, hh * NS + (NS * C_SA - NS + 3))
                    apart()
                    A(qh[:, :], area[:, ds(q_slot, 1), :], ACT.Copy, scale=SCALE).then_inc(qk_hi, 1)
                    A(kh[:, :], area[:, ds(k_slot, 1), :], ACT.Copy).then_inc(qk_hi, 1)
                return f

            def v_high(hh):
                act.wait_ge(v_turned, hh + 1)
                A(vh[:, :], attn[3][:, :], ACT.Copy).then_inc(v_hi, 1)

            def gate_exp_z(hh, z_slot):
                act.wait_ge(v_staged, hh + 1)
                apart()
                A(og[:, :], area[:, ds(z_slot, 1), :], ACT.Exp, scale=-1.0).then_inc(gate_exp, 1)

            def sb_steps(n):
                def e_tile(i):
                    w = WK[i]
                    act.wait_ge(z_done, n * 4 + i + 1)
                    if i >= 2:
                        act.wait_ge(sp_ready, n * 4 + i - 1)
                    t = eb[:, i % 2, 0:w]
                    A(t, attn[i][:, 0:w], ACT.Abs).then_inc(e_step, 1)
                    act.wait_ge(e_step, n * 8 + 2 * i + 1)
                    A(t, t, ACT.Exp, scale=-1.0).then_inc(e_step, 1)
                    act.wait_ge(e_step, n * 8 + 2 * i + 2)
                    A(t, t, ACT.Ln, bias=1.0).then_inc(e_ready, 1)

                def sp_high(i):
                    act.wait_ge(sp_ready, n * 4 + i + 1)
                    A(x_hi[:, OK[i]:OK[i] + WK[i]], full[:, i % 2, 0:WK[i]], ACT.Copy).then_inc(sp_hi, 1)

                def weights(i):
                    w = WK[i]
                    if i == 0:
                        act.wait_ge(c_done, n * 4 + 4)
                    if i >= 2:
                        act.wait_ge(w_low, n * 4 + i - 1)
                    A(full[:, i % 2, 0:w], attn[i][:, 0:w], ACT.Exp).then_inc(w_full, 1)
                    A(x_hi[:, OK[i]:OK[i] + w], attn[i][:, 0:w], ACT.Exp).then_inc(w_full, 1)

                def s1():
                    v_high(n)
                    e_tile(0)
                    e_tile(1)

                def s2():
                    sp_high(0)
                    e_tile(2)
                    sp_high(1)

                def s3():
                    e_tile(3)
                    sp_high(2)
                    sp_high(3)

                def s5():
                    weights(0)
                    weights(1)

                def s6():
                    weights(2)
                    weights(3)

                return [stage_qk(n, n, n + HEADS), s1, s2, s3,
                        lambda: gate_exp_z(n, n + 3 * HEADS), s5, s6]

            with act.Fori(0, HEADS) as n:
                c = n + C_SA
                chunk(c, sb_steps(n))
                act.wait_ge(v_staged, n + 1)
                act.wait_ge(qk_lo, n * 2 + 2)
                act.wait_ge(silu_step, n * 3 + 3)
                evacuate(c, lambda e: area[:, ds(n + 8 * e, 1), :])

            def sa_steps(n, slot):
                hh = n + HEADS

                def probs(i):
                    act.wait_ge(max_ready, n * 4 + i + 1)
                    t = p_sa[:, OQ[i]:OQ[i] + WQ[i]]
                    A(t, t, ACT.Exp, bias=nmax[:, i:i + 1],
                      accum_out=psum_p[:, i:i + 1]).then_inc(p_exp, 1)

                def turned_high(i):
                    if i == 0:
                        act.wait_ge(pt_done, n * 4 + 4)
                    A(x_hi[:, OK[i]:OK[i] + WK[i]], attn[i][:, 0:WK[i]], ACT.Copy).then_inc(pt_hi, 1)

                def s2():
                    probs(0)
                    probs(1)

                def s3():
                    probs(2)
                    probs(3)

                def s5():
                    for i in range(QT):
                        turned_high(i)

                return [stage_qk(hh, slot(0), slot(1)), lambda: v_high(hh), s2, s3,
                        lambda: gate_exp_z(hh, slot(3)), s5]

            with act.Fori(0, 2) as a:
                with act.Fori(0, 4) as b:
                    n = a * 4 + b
                    chunk(n + C_GATE, sa_steps(n, lambda kind: b * 8 + a + 2 * kind))
                    act.wait_ge(v_staged, n + HEADS + 1)
                    act.wait_ge(qk_lo, n * 2 + 2 * HEADS + 2)
                    act.wait_ge(silu_step, n * 3 + 3 * HEADS + 3)
                    evacuate(n + C_GATE, lambda e: area[:, ds(b * 8 + a + 2 * e, 1), :])

            def o_high(ts):
                def f():
                    for t in ts:
                        if t % 4 == 0:
                            act.wait_ge(o_loaded[t // 4], 16)
                        if t == 0:
                            act.wait_ge(strip_used, NS * C_BRANCH)
                        A(u_hi[:, t, :], returned(t), ACT.Copy).then_inc(o_hi, 1)
                return f

            def sigmoid_steps(c):
                def f(e):
                    def g():
                        t = area[:, 8 * (c - C_BRANCH) + 2 * e:8 * (c - C_BRANCH) + 2 * e + 2, :] \
                            if isinstance(c, int) else area[:, ds(c * 8 + (2 * e - 8 * C_BRANCH), 2), :]
                        A(t, t, ACT.Sigmoid).then_inc(sigmoid_ready, 1)
                    return g
                return [f(e) for e in range(4)]

            def mix_high(c):
                for e in range(4):
                    d = c * 4 + (e - 4 * C_BRANCH)
                    act.wait_ge(mix_ready, d + 1)
                    apart()
                    A(area_r[:, ds(d * 2, 1), :], mix[:, e, :], ACT.Copy).then_inc(mix_hi, 1)

            o_high(range(0, 4))()
            sig = sigmoid_steps(C_BRANCH)
            chunk(C_BRANCH, [o_high(range(4, 8)), o_high(range(8, 12)), sig[0], o_high(range(12, 16)),
                             sig[1], sig[2], sig[3]])
            for e in range(4):
                act.wait_ge(mix_ready, e + 1)
                A(area_r[:, 2 * e, :], mix[:, e, :], ACT.Copy).then_inc(mix_hi, 1)
            with act.Fori(C_BRANCH + 1, C_OUT) as c:
                chunk(c, sigmoid_steps(c))
                mix_high(c)

            def squares(c, tiles=range(QT)):
                m = c - C_OUT
                for i in tiles:
                    act.wait_ge(h_ready, m * 4 + i + 1)
                    src = hres[:, i, CW * m:CW * m + CW] if isinstance(c, int) else hres[:, i, ds(m * CW, CW)]
                    acc = ssq[:, i, m:m + 1] if isinstance(c, int) else ssq[:, i, ds(m, 1)]
                    if 4 * m + i >= 2:
                        act.wait_ge(sq_done, m * 4 + i - 1)
                    A(junk2[:, i % 2, :], src, ACT.Square, accum_out=acc).then_inc(sq_done, 1)

            for c in range(C_OUT, C_LAST):
                chunk(c)
                if c == C_LAST - 1:
                    for s in range(LEAD, SHARED):
                        split_hi(C_LAST, s)
                squares(c)
            for s in range(SHARED, NS):
                t = 2 * (s - SHARED)
                act.wait_ge(strip_loaded[s % 2], 16 * (C_LAST * NS // 2 + s // 2 + 1))
                A(last_hi[:, t:t + 2, :], stage[:, s % 2, :, :], ACT.Copy).then_inc(strip_hi, 1)
            nc.scalar.preload_act_table_set("sqrt_and_others")
            for i in range(QT):
                squares(C_LAST, (i,))
                act.wait_ge(norm_step, 6 * QT + 7 * i + 2)
                A(root[:, i:i + 1], var[:, i:i + 1], ACT.Sqrt).then_inc(rooted, 1)
                act.wait_ge(norm_step, 6 * QT + 7 * i + 7)
                act.wait_ge(hg_ready, 4 * (C_LAST - C_OUT) + i + 1)
                t = hres[:, i, YV:D_MODEL]
                A(t, t, ACT.Copy, scale=rstd[:, i:i + 1]).then_inc(y_ready[1], 1)

        @block.vector
        def _(dve):
            V = nc.vector

            def split_lo(c, s):
                dve.wait_ge(strip_hi, c * NS + (s + 1))
                V.tensor_tensor(w_lo[:, s % RING, :, :], stage[:, s % 2, :, :],
                                w_hi[:, s % RING, :, :].bitcast(F), ALU.subtract).then_inc(strip_lo, 1)

            def chunk(c, steps=()):
                for s in range(NS):
                    split_lo(c, s + LEAD)
                    if s < len(steps) and steps[s]:
                        steps[s]()

            def rsqrt(cols, k, first):
                def step(ins):
                    ins.then_inc(norm_step, 1)
                v_, r_, t_, y_, s_ = (t[:, cols] for t in (var, root, tmp, rinv, ss))
                step(V.tensor_scalar(v_, s_, 1.0 / D_MODEL, EPS, ALU.mult, ALU.add))
                dve.wait_ge(rooted, k)
                step(V.reciprocal(y_, r_))
                dve.wait_ge(norm_step, first + 2)
                step(V.tensor_tensor(t_, y_, y_, ALU.mult))
                dve.wait_ge(norm_step, first + 3)
                step(V.tensor_tensor(t_, t_, v_, ALU.mult))
                dve.wait_ge(norm_step, first + 4)
                step(V.tensor_scalar(t_, t_, -0.5, 1.5, ALU.mult, ALU.add))
                dve.wait_ge(norm_step, first + 5)
                step(V.tensor_tensor(rstd[:, cols], y_, t_, ALU.mult))

            for h in range(HEADS):
                V.memset(slope[:, h:h + 1], -(2.0 ** (-8.0 * (h + 1) / HEADS)))
            dve.wait_ge(masks, 3)
            V.tensor_scalar(big_ident[:, :], ident[:, :], BIG, None, ALU.mult)
            V.tensor_copy(neg_tri[:, :], cst[:, 0, :])
            V.tensor_copy(neg_one[:, :], cst[:, 1, :]).then_inc(consts, 1)

            def turned_u_low(i):
                for j in range(4):
                    dve.wait_ge(u_hi_ready, 4 * i + j + 1)
                    V.tensor_tensor(u_lo[:, 4 * j:4 * j + 4, P * i:P * i + P],
                                    attn[j][:, :].rearrange("p (t s) -> p t s", t=4),
                                    u_hi[:, 4 * j:4 * j + 4, P * i:P * i + P].bitcast(F),
                                    ALU.subtract).then_inc(u_lo_ready, 1)

            for i in range(QT):
                dve.wait_ge(sumsq, i + 1)
                rsqrt(slice(i, i + 1), i + 1, 6 * i)
                dve.wait_ge(norm_step, 6 * i + 6)
                if i < 2:
                    dve.wait_ge(gain_loaded, 16)
                    V.scalar_tensor_tensor(xg[:, i, :], xs[:, i, :], rstd[:, i:i + 1], gain[:, :],
                                           ALU.mult, ALU.mult).then_inc(xn_ready, 1)
                else:
                    dve.wait_ge(xg_ready, i - 1)
                    V.tensor_scalar(xg[:, i, :], xg[:, i, :], rstd[:, i:i + 1], None,
                                    ALU.mult).then_inc(xn_ready, 1)
                if i == QT - 1:
                    dve.wait_ge(ixw_hi_ready, 1)
                    V.tensor_tensor(ixw_lo[:, :, :], ixw[:, :, :], ixw_hi[:, :, :].bitcast(F),
                                    ALU.subtract).then_inc(ixw_lo_ready, 1)
                if i:
                    turned_u_low(i - 1)
            turned_u_low(QT - 1)
            for s in range(LEAD):
                split_lo(0, s)
            dve.wait_ge(kix_hi_ready, 2)
            dve.wait_ge(kw_copied, 1)
            for rows_ in HALVES:
                V.tensor_tensor(kix_lo[rows_, :], proj[3][0:IDX_DIM, :], kix_hi[0:IDX_DIM, :].bitcast(F),
                                ALU.subtract).then_inc(kix_lo_ready, 1)
            dve.wait_ge(far_ready, 1)
            V.memset(far[0:P // 2, P // 2:P], BIG)
            dve.wait_ge(wix_turned, 1)
            V.tensor_scalar(wix[:, :, :],
                            attn[0][:, 0:QT * KW].rearrange("p (i e) -> p i e", i=QT)[:, :, IDX_DIM:KW],
                            IDX_HEADS ** -0.5 * IDX_DIM ** -0.5, None, ALU.mult).then_inc(wix_ready, 1)

            for c in range(C_QIX, C_SB):
                chunk(c)
                for e in range(4):
                    dve.wait_ge(qix_hi_ready, 8 * c + 2 * e + 2)
                    for par, rows_ in enumerate(HALVES):
                        h = 16 + 8 * c + 2 * e + par
                        m = V.tensor_tensor(area_r[HALVES[1 - par], h, :], proj[e][rows_, :],
                                            area_r[rows_, h, :].bitcast(F), ALU.subtract)
                    m.then_inc(proj_free, 1)

            def score_step(qi, s):
                w = WQ[qi]
                acc = score[:, qi % 2, 0:w]
                for h in (2 * s, 2 * s + 1):
                    n = IDX_HEADS * (qi - 1) + h
                    dve.wait_ge(relu_ready, n + 1)
                    if h == 0:
                        if n == 0:
                            dve.wait_ge(wix_ready, 1)
                        V.tensor_scalar(acc, relu[:, n % 2, 0:w], wix[:, qi, h:h + 1], None,
                                        ALU.mult).then_inc(relu_used, 1)
                    else:
                        dve.wait_ge(relu_used, n)
                        V.scalar_tensor_tensor(acc, relu[:, n % 2, 0:w], wix[:, qi, h:h + 1], acc,
                                               ALU.mult, ALU.add).then_inc(relu_used, 1)
                if s == NS - 1:
                    dve.wait_ge(relu_used, IDX_HEADS * qi)
                    V.memset(score[0:P // 2, qi % 2, w - P // 2:w], HIDDEN).then_inc(pick_step, 1)

            ROUNDS = TOPK // 8
            PICK = 2 * ROUNDS + 2

            def pick_round(qi, r):
                w = WQ[qi]
                acc = score[:, qi % 2, 0:w]
                base = PICK * (qi - 1) + 2 * r + 1
                dve.wait_ge(pick_step, base)
                V.max(top8[:, :], acc).then_inc(pick_step, 1)
                dve.wait_ge(pick_step, base + 1)
                V.match_replace(acc, top8[:, :], acc, TAKEN).then_inc(pick_step, 1)
                if r == ROUNDS - 1:
                    dve.wait_ge(pick_step, base + 2)
                    V.tensor_scalar(acc, acc, TAKEN, BIG, ALU.not_equal, ALU.mult).then_inc(pick_step, 1)
                    dve.wait_ge(pick_step, base + 3)
                    t = far[:, OQ[qi]:OQ[qi] + w]
                    V.tensor_tensor(t, t, acc, ALU.add).then_inc(far_ready, 1)

            for c in range(C_SB, C_SB + 4):
                qi = c - C_SB + 1

                def step(s, qi=qi):
                    def f():
                        if qi >= 2:
                            for r in range(ROUNDS // NS):
                                pick_round(qi - 1, ROUNDS // NS * s + r)
                        if qi < QT:
                            score_step(qi, s)
                    return f

                chunk(c, [step(s) for s in range(NS)])
            with dve.Fori(C_SB + 4, C_SA) as c:
                chunk(c)

            def qk_low(hh, q_slot, k_slot):
                def f():
                    dve.wait_ge(qk_hi, hh * 2 + 2)
                    V.scalar_tensor_tensor(ql[:, :], area[:, ds(q_slot, 1), :], SCALE, qh[:, :].bitcast(F),
                                           ALU.mult, ALU.subtract).then_inc(qk_lo, 1)
                    V.tensor_tensor(kl[:, :], area[:, ds(k_slot, 1), :], kh[:, :].bitcast(F),
                                    ALU.subtract).then_inc(qk_lo, 1)
                return f

            def v_low(hh):
                dve.wait_ge(v_hi, hh + 1)
                V.tensor_tensor(vl[:, :], attn[3][:, :], vh[:, :].bitcast(F), ALU.subtract).then_inc(v_lo, 1)

            def silu(hh, z_slot):
                dve.wait_ge(gate_exp, hh + 1)
                V.tensor_scalar(og[:, :], og[:, :], 1.0, None, ALU.add).then_inc(silu_step, 1)
                dve.wait_ge(silu_step, hh * 3 + 1)
                V.reciprocal(og[:, :], og[:, :]).then_inc(silu_step, 1)
                dve.wait_ge(silu_step, hh * 3 + 2)
                V.tensor_tensor(og[:, :], og[:, :], area[:, ds(z_slot, 1), :], ALU.mult).then_inc(silu_step, 1)

            def gated(hh):
                dve.wait_ge(av_done, hh + 1)
                dve.wait_ge(silu_step, hh * 3 + 3)
                V.tensor_tensor(og[:, :], attn[0][:, :], og[:, :], ALU.mult).then_inc(o_ready, 1)

            def sb_steps(n):
                def softplus(i):
                    w = WK[i]
                    dve.wait_ge(e_ready, n * 4 + i + 1)
                    if i >= 2:
                        dve.wait_ge(sp_lo, n * 4 + i - 1)
                    V.scalar_tensor_tensor(full[:, i % 2, 0:w], attn[i][:, 0:w], 0.0, eb[:, i % 2, 0:w],
                                           ALU.max, ALU.add).then_inc(sp_step, 1)
                    dve.wait_ge(sp_step, n * 4 + i + 1)
                    t = full[:, i % 2, 0:P]
                    V.tensor_tensor(t, t, before[:, :], ALU.mult).then_inc(sp_ready, 1)

                def sp_low(i):
                    w = WK[i]
                    dve.wait_ge(sp_hi, n * 4 + i + 1)
                    V.tensor_tensor(x_lo[:, OK[i]:OK[i] + w], full[:, i % 2, 0:w],
                                    x_hi[:, OK[i]:OK[i] + w].bitcast(F), ALU.subtract).then_inc(sp_lo, 1)

                def weights_low(i):
                    w = WK[i]
                    dve.wait_ge(w_full, n * 8 + 2 * i + 2)
                    V.tensor_tensor(x_lo[:, OK[i]:OK[i] + w], full[:, i % 2, 0:w],
                                    x_hi[:, OK[i]:OK[i] + w].bitcast(F), ALU.subtract).then_inc(w_low, 1)

                def s1():
                    v_low(n)
                    softplus(0)
                    softplus(1)

                def s2():
                    sp_low(0)
                    softplus(2)
                    sp_low(1)

                def s3():
                    softplus(3)
                    sp_low(2)
                    sp_low(3)

                def s5():
                    weights_low(0)
                    weights_low(1)

                def s6():
                    weights_low(2)
                    weights_low(3)

                return [qk_low(n, n, n + HEADS), s1, s2, s3,
                        lambda: silu(n, n + 3 * HEADS), s5, s6, lambda: gated(n)]

            with dve.Fori(0, HEADS) as n:
                chunk(n + C_SA, sb_steps(n))

            def sa_steps(n, slot):
                hh = n + HEADS

                def logits(i):
                    w = WQ[i]
                    t = p_sa[:, OQ[i]:OQ[i] + w]
                    dve.wait_ge(z_done, hh * 4 + i + 1)
                    V.scalar_tensor_tensor(t, far[:, OQ[i]:OQ[i] + w], slope[:, ds(n, 1)], attn[i][:, 0:w],
                                           ALU.mult, ALU.add).then_inc(lg_ready, 1)
                    dve.wait_ge(lg_ready, n * 4 + i + 1)
                    V.tensor_reduce(nmax[:, i:i + 1], t, AX.X, ALU.max, negate=True).then_inc(max_ready, 1)

                def normalize(i):
                    dve.wait_ge(p_exp, n * 4 + i + 1)
                    V.reciprocal(pinv[:, i:i + 1], psum_p[:, i:i + 1]).then_inc(inv_ready, 1)
                    dve.wait_ge(inv_ready, n * 4 + i + 1)
                    t = p_sa[:, OQ[i]:OQ[i] + WQ[i]]
                    V.tensor_scalar(t, t, pinv[:, i:i + 1], None, ALU.mult).then_inc(p_ready, 1)

                def turned_low(i):
                    dve.wait_ge(pt_hi, n * 4 + i + 1)
                    V.tensor_tensor(x_lo[:, OK[i]:OK[i] + WK[i]], attn[i][:, 0:WK[i]],
                                    x_hi[:, OK[i]:OK[i] + WK[i]].bitcast(F), ALU.subtract).then_inc(w_low, 1)

                def s1():
                    v_low(hh)
                    logits(0)
                    logits(1)

                def s2():
                    logits(2)
                    logits(3)

                def s3():
                    normalize(0)
                    normalize(1)

                def s4():
                    normalize(2)
                    normalize(3)
                    silu(hh, slot(3))

                def s5():
                    for i in range(QT):
                        turned_low(i)

                return [qk_low(hh, slot(0), slot(1)), s1, s2, s3, s4, s5, None, lambda: gated(hh)]

            dve.wait_ge(far_ready, QT)
            with dve.Fori(0, 2) as a:
                with dve.Fori(0, 4) as b:
                    n = a * 4 + b
                    chunk(n + C_GATE, sa_steps(n, lambda kind: b * 8 + a + 2 * kind))

            def o_low(ts):
                def f():
                    for t in ts:
                        dve.wait_ge(o_hi, t + 1)
                        V.tensor_tensor(u_lo[:, t, :], returned(t), u_hi[:, t, :].bitcast(F),
                                        ALU.subtract).then_inc(o_lo, 1)
                return f

            def slot_of(c, e, lo):
                if isinstance(c, int):
                    return slice(8 * (c - C_BRANCH) + 2 * e + lo, 8 * (c - C_BRANCH) + 2 * e + lo + 1)
                return ds(c * 8 + (2 * e + lo - 8 * C_BRANCH), 1)

            def mix_sb(c):
                m = c - C_BRANCH

                def f():
                    for e in range(4):
                        bank_done(dve, c, e, strips=NS // 2)
                        dve.wait_ge(sigmoid_ready, m * 4 + e + 1)
                        V.tensor_tensor(mix[:, e, :], proj[e][:, :], area[:, slot_of(c, e, 0), :],
                                        ALU.mult).then_inc(proj_free, 1)
                return f

            def mix_both(c):
                m = c - C_BRANCH
                for e in range(4):
                    bank_done(dve, c, e, done=branch_sa_done, m=m)
                    if not (isinstance(c, int) and e == 0):
                        dve.wait_ge(mix_ready, m * 4 + e)
                    V.tensor_tensor(mix_sa[:, :], attn[e][:, :], area[:, slot_of(c, e, 1), :],
                                    ALU.mult).then_inc(attn_free, 1)
                    dve.wait_ge(attn_free, m * 4 + e + 1)
                    if e == 0:
                        dve.wait_ge(proj_free, c * 4 + 4)
                    V.tensor_tensor(mix[:, e, :], mix[:, e, :], mix_sa[:, :], ALU.add).then_inc(mix_ready, 1)
                for e in range(4):
                    dve.wait_ge(mix_hi, m * 4 + e + 1)
                    V.tensor_tensor(area_r[:, slot_of(c, e, 1), :], mix[:, e, :],
                                    area_r[:, slot_of(c, e, 0), :].bitcast(F), ALU.subtract).then_inc(mix_lo, 1)

            o_low(range(0, 4))()
            chunk(C_BRANCH, [o_low(range(4, 8)), o_low(range(8, 12)), None, o_low(range(12, 16)),
                             None, mix_sb(C_BRANCH)])
            mix_both(C_BRANCH)
            with dve.Fori(C_BRANCH + 1, C_OUT) as c:
                chunk(c, [None, None, None, None, None, mix_sb(c)])
                mix_both(c)

            def residual(c, tiles=range(QT), done=bank_done):
                m = c - C_OUT
                sl = slice(CW * m, CW * m + CW)
                for i in tiles:
                    t = hres[:, i, sl]
                    done(dve, c, i)
                    V.tensor_tensor(t, proj[i][:, :], t, ALU.add).then_inc(h_ready, 1)
                for i in tiles:
                    t = hres[:, i, sl]
                    dve.wait_ge(sq_done, m * 4 + i + 1)
                    V.tensor_tensor(t, t, fgain[:, sl], ALU.mult).then_inc(hg_ready, 1)

            for c in range(C_OUT, C_LAST):
                chunk(c)
                if c == C_LAST - 1:
                    for s in range(LEAD, SHARED):
                        split_lo(C_LAST, s)
                if c == C_OUT:
                    dve.wait_ge(res_loaded, 16)
                    dve.wait_ge(fgain_loaded, 16)
                residual(c)
            for s in range(SHARED, NS):
                t = 2 * (s - SHARED)
                dve.wait_ge(strip_hi, NS * C_LAST + s + 1)
                V.tensor_tensor(last_lo[:, t:t + 2, :], stage[:, s % 2, :, :],
                                last_hi[:, t:t + 2, :].bitcast(F), ALU.subtract).then_inc(strip_lo, 1)
            for i in range(QT):
                residual(C_LAST, (i,), lambda eng, c, i: eng.wait_ge(last_done, i + 1))
                V.tensor_reduce(ss[:, i:i + 1], ssq[:, i, :], AX.X, ALU.add).then_inc(norm_step, 1)
                dve.wait_ge(norm_step, 6 * QT + 7 * i + 1)
                rsqrt(slice(i, i + 1), QT + i + 1, 6 * QT + 7 * i + 1)
                dve.wait_ge(norm_step, 6 * QT + 7 * i + 7)
                dve.wait_ge(hg_ready, 4 * (C_LAST - C_OUT) + i + 1)
                t = hres[:, i, 0:YV]
                V.tensor_scalar(t, t, rstd[:, i:i + 1], None, ALU.mult).then_inc(y_ready[0], 1)

        @block.tensor
        def _(pe):
            def mm3(out_, a_hi, a_lo, b_hi, b_lo, start, stop, free=False):
                nc.tensor.matmul(out_, a_hi, b_hi, start=start, stop=False, skip_group_check=free)
                nc.tensor.matmul(out_, a_hi, b_lo, start=False, stop=False, skip_group_check=free)
                return nc.tensor.matmul(out_, a_lo, b_hi, start=False, stop=stop, skip_group_check=free)

            def strip(c, s, first, last, tokens=False, banks=proj, free_of=None, done=proj_done,
                      ready=None):
                pe.wait_ge(strip_lo, c * NS + (s + 1))
                if ready:
                    ready(2 * s + 1)
                for e in range(4):
                    for j in range(2):
                        t = 2 * s + j
                        st, en = first and j == 0, last and j == 1
                        if st and free_of is not None:
                            free_of(e)
                        cols = slice(P * e, P * e + P)
                        r = s % RING
                        if tokens:
                            m = mm3(banks[e][:, :], area_r[:, 2 * t, cols], area_r[:, 2 * t + 1, cols],
                                    w_hi[:, r, j, :], w_lo[:, r, j, :], st, en)
                        else:
                            m = mm3(banks[e][:, :], w_hi[:, r, j, cols], w_lo[:, r, j, cols],
                                    u_hi[:, t, :], u_lo[:, t, :], st, en)
                        if en and e < 3:
                            m.then_inc(done, 1)
                m.then_inc(strip_used, 1)

            def chunk(c, steps=(), tokens=False, ready=None):
                def bank_free(e):
                    if tokens and not isinstance(c, int):
                        pe.wait_ge(h_ready, c * 4 + (e - 3 - 4 * C_OUT))
                    elif not (isinstance(c, int) and c == 0):
                        pe.wait_ge(proj_free, c * 4 + (e - 3))
                    elif e == 3:
                        pe.wait_ge(kix_lo_ready, 2)
                for s in range(NS):
                    strip(c, s, s == 0, s == NS - 1, tokens, free_of=bank_free, ready=ready)
                    if s < len(steps) and steps[s]:
                        steps[s]()

            def turn_x(i):
                pe.wait_ge(xn_ready, i + 1)
                for j in range(4):
                    if i > 0:
                        pe.wait_ge(u_lo_ready, 4 * (i - 1) + j + 1)
                    for t in range(4):
                        k = 4 * j + t
                        m = nc.tensor.transpose(attn[j][:, P * t:P * t + P], xg[:, i, P * k:P * k + P], ident[:, :])
                    m.then_inc(xt_done, 1)

            def index_keys(i):
                cols = slice(P * i, P * i + P)
                for t in range(KT):
                    if t % 4 == 0:
                        pe.wait_ge(u_lo_ready, 4 * i + t // 4 + 1)
                    m = mm3(proj[3][0:KW, cols], ixw_hi[:, t, :], ixw_lo[:, t, :],
                            u_hi[:, t, cols], u_lo[:, t, cols], t == 0, t == KT - 1)
                if i == QT - 1:
                    m.then_inc(kw_done, 1)

            pe.wait_ge(masks, 1)
            for i in range(QT - 1):
                turn_x(i)
            pe.wait_ge(ixw_lo_ready, 1)
            index_keys(0)
            turn_x(QT - 1)
            for i in range(1, QT):
                index_keys(i)

            def turn_wix():
                pe.wait_ge(kw_copied, 1)
                for i in range(QT):
                    m = nc.tensor.transpose(attn[0][:, KW * i:KW * i + KW], kw_t[0:KW, P * i:P * i + P],
                                            ident[0:KW, 0:KW])
                m.then_inc(wix_turned, 1)

            chunk(C_QIX, [turn_wix])
            for c in range(C_QIX + 1, C_SB):
                chunk(c)

            def dots(qi, s):
                def f():
                    for h in (2 * s, 2 * s + 1):
                        n = IDX_HEADS * (qi - 1) + h
                        if n == 0:
                            pe.wait_ge(kix_lo_ready, 2)
                            pe.wait_ge(wix_ready, 1)
                            pe.wait_ge(proj_free, 4 * C_SB)
                        if n >= 4:
                            pe.wait_ge(relu_ready, n - 3)
                        q = area_r[:, 16 + h, P * qi:P * qi + P]
                        o_ = attn[h % 4][:, 0:WQ[qi]]
                        nc.tensor.matmul(o_, q, kix_lo[:, 0:WQ[qi]], start=True, stop=False)
                        nc.tensor.matmul(o_, q, kix_hi[:, 0:WQ[qi]], start=False, stop=True).then_inc(dots_done, 1)
                return f

            for c in range(C_SB, C_SB + 4):
                qi = c - C_SB + 1
                chunk(c, [dots(qi, s) for s in range(NS)] if qi < QT else ())
            with pe.Fori(C_SB + 4, C_SA) as c:
                chunk(c)

            def turn_v(hh):
                pe.wait_ge(v_staged, hh + 1)
                for i in range(QT):
                    m = nc.tensor.transpose(attn[3][:, P * i:P * i + P], v_t[:, P * i:P * i + P], ident[:, :])
                m.then_inc(v_turned, 1)

            def times_v(hh):
                pe.wait_ge(w_low, hh * 4 + 4)
                for i in range(QT):
                    k = slice(OK[i], OK[i] + WK[i])
                    v = slice(P * i, P * i + P)
                    m = mm3(attn[0][:, P * i:SEQ], vh[:, v], vl[:, v], x_hi[:, k], x_lo[:, k],
                            i == 0, i == QT - 1)
                m.then_inc(av_done, 1)

            def sb_steps(n):
                def z(i):
                    k = slice(P * i, P * i + P)
                    mm3(attn[i][:, 0:WK[i]], kh[:, k], kl[:, k], qh[:, P * i:SEQ], ql[:, P * i:SEQ],
                        True, True, True).then_inc(z_done, 1)

                def s0():
                    turn_v(n)
                    pe.wait_ge(qk_lo, n * 2 + 2)
                    for i in range(3):
                        z(i)

                def s1():
                    pe.wait_ge(v_lo, n + 1)
                    z(3)

                def s4():
                    pe.wait_ge(sp_lo, n * 4 + 4)
                    for i in range(QT):
                        for j in range(i, QT):
                            o_ = attn[i][:, P * (j - i):WK[i]]
                            a = neg_tri if i == j else neg_one
                            for part in (x_lo, x_hi):
                                nc.tensor.matmul(o_, a[:, :], part[:, OK[j]:OK[j] + WK[j]],
                                                 start=False, stop=False, skip_group_check=True)
                        nc.tensor.matmul(attn[i][:, 0:P], big_ident[:, :], neg_tri[:, :], start=False, stop=True,
                                         skip_group_check=True).then_inc(c_done, 1)

                return [s0, s1, None, None, s4, None, lambda: times_v(n)]

            pe.wait_ge(consts, 5)
            with pe.Fori(0, HEADS) as n:
                chunk(n + C_SA, sb_steps(n))

            def sa_steps(n):
                hh = n + HEADS

                def lg(i):
                    q = slice(P * i, P * i + P)
                    mm3(attn[i][:, 0:WQ[i]], qh[:, q], ql[:, q], kh[:, 0:WQ[i]], kl[:, 0:WQ[i]],
                        True, True).then_inc(z_done, 1)

                def s0():
                    turn_v(hh)
                    pe.wait_ge(qk_lo, hh * 2 + 2)
                    for i in range(3):
                        lg(i)

                def s1():
                    pe.wait_ge(v_lo, hh + 1)
                    lg(3)

                def s4():
                    pe.wait_ge(p_ready, n * 4 + 4)
                    for i in range(QT):
                        for q in range(i, QT):
                            m = nc.tensor.transpose(attn[i][:, P * (q - i):P * (q - i) + P],
                                                    p_sa[:, OQ[q] + P * i:OQ[q] + P * i + P], ident[:, :])
                        m.then_inc(pt_done, 1)

                return [s0, s1, None, None, s4, None, lambda: times_v(hh)]

            with pe.Fori(0, 2) as a:
                with pe.Fori(0, 4) as b:
                    n = a * 4 + b
                    chunk(n + C_GATE, sa_steps(n))

            def branch_chunk(c):
                m_ = c - C_BRANCH

                def sb_free(e):
                    pe.wait_ge(proj_free, c * 4 + (e - 3))

                def sa_free(e):
                    if isinstance(c, int):
                        pe.wait_ge(o_ready, 2 * HEADS)
                    else:
                        pe.wait_ge(attn_free, m_ * 4 + (e - 3))

                ready = (lambda t: pe.wait_ge(o_lo, t + 1)) if isinstance(c, int) else None
                for s in range(NS):
                    h = NS // 2
                    if s < h:
                        strip(c, s, s == 0, s == h - 1, free_of=sb_free, ready=ready)
                    else:
                        strip(c, s, s == h, s == NS - 1, banks=attn, free_of=sa_free, done=branch_sa_done,
                              ready=ready)

            branch_chunk(C_BRANCH)
            with pe.Fori(C_BRANCH + 1, C_OUT) as c:
                branch_chunk(c)

            chunk(C_OUT, tokens=True, ready=lambda t: pe.wait_ge(mix_lo, t + 1))
            with pe.Fori(C_OUT + 1, C_LAST) as c:
                chunk(c, tokens=True)
            for s in range(SHARED):
                strip(C_LAST, s, s == 0, False, tokens=True,
                      free_of=lambda e: pe.wait_ge(h_ready, 4 * (C_LAST - 1 - C_OUT) + e + 1))
            for i in range(QT):
                for t in range(2 * SHARED, KT):
                    if i == 0 and t % 2 == 0:
                        pe.wait_ge(strip_lo, NS * C_LAST + t // 2 + 1)
                    cols = slice(P * i, P * i + P)
                    m = mm3(proj[i][:, :], area_r[:, 2 * t, cols], area_r[:, 2 * t + 1, cols],
                            last_hi[:, t - 2 * SHARED, :], last_lo[:, t - 2 * SHARED, :], False, t == KT - 1)
                m.then_inc(last_done, 1)


_INS = ["x", "norm_gain", "w_in", "w_branch_sb", "w_branch_sa", "w_out", "final_norm_gain"]


def kernel(**inputs):
    import numpy as np
    import concourse.bacc as bacc
    from concourse.bass_utils import run_bass_kernel_spmd

    nc = bacc.Bacc("TRN2", target_bir_lowering=False, num_devices=1,
                   dynamic_dma_scratch_size=8192)
    arrays, args = {}, []
    for name in _INS:
        a = np.ascontiguousarray(inputs[name])
        arrays[f"in_{name}"] = a
        args.append(nc.dram_tensor(f"in_{name}", a.shape, mybir.dt.from_np(a.dtype), kind="ExternalInput").ap())
    args.append(nc.dram_tensor("out_h", (1, SEQ, D_MODEL), mybir.dt.float32, kind="ExternalOutput").ap())
    build(nc, *args)
    r = run_bass_kernel_spmd(nc, [arrays], core_ids=[0])
    return r.results[0]["out_h"]
```

```python
from contextlib import ExitStack

import concourse.bass as bass
from concourse import mybir

D_MODEL, SEQ = 2048, 512
HEADS, HD = 8, 128
IDX_HEADS, IDX_DIM = 16, 64
TOPK = min(256, SEQ // 4)
EPS = 1e-6
P = 128
QT = SEQ // P
KT = D_MODEL // P
CW = 512
NS = KT // 2
RING = 4
LEAD = 2
BIG = 1e30
HIDDEN, TAKEN = -3.0e38, -3.4e38

COL_SB = 0
COL_QIX = 8 * HEADS * HD
COL_KIX = COL_QIX + IDX_HEADS * IDX_DIM
KW = IDX_DIM + IDX_HEADS
COL_GATE = COL_KIX + KW

C_QIX, C_SB, C_SA, C_GATE, C_BRANCH, C_OUT, C_END = 0, 2, 10, 18, 26, 30, 34
C_LAST = C_END - 1
SHARED = 3

WK = [SEQ - P * i for i in range(QT)]
OK = [sum(WK[:i]) for i in range(QT)]
WQ = [P * (i + 1) for i in range(QT)]
OQ = [sum(WQ[:i]) for i in range(QT)]
TRI = sum(WK)
SMALL = 1024


def build(nc, x, norm_gain, w_in, w_branch_sb, w_branch_sa, w_out, final_gain, out):
    F, R, I = mybir.dt.float32, mybir.dt.float32r, mybir.dt.int32
    ALU, ACT, AX = mybir.AluOpType, mybir.ActivationFunctionType, mybir.AxisListType
    ds = bass.ds

    place = {}

    def at(name, shape, dt, offset):
        return nc.alloc_sbuf_tensor_at(name, [P] + shape, dt, offset=offset)

    top = [(nc.sbuf_base + 31) // 32 * 32]

    def region(name, size):
        place[name] = top[0]
        top[0] += size
        return place[name]

    TILE = 4 * SEQ
    region("u_hi", KT * TILE)
    region("u_lo", KT * TILE)
    region("area", 32 * TILE)
    region("stage", 2 * 2 * TILE)
    region("w_hi", RING * 2 * TILE)
    region("w_lo", RING * 2 * TILE)
    work = region("work", 11 * TILE + 2 * 4 * TRI)
    region("small", SMALL)
    region("far", 4 * TRI)
    region("const", 5 * 4 * P)
    region("late", 5 * 1024)
    assert top[0] <= nc.sbuf_usable_end, top[0]

    u_hi = at("u_hi", [KT, SEQ], R, place["u_hi"])
    u_lo = at("u_lo", [KT, SEQ], R, place["u_lo"])
    hres = at("hres", [QT, D_MODEL], F, place["u_hi"])
    area = at("area", [32, SEQ], F, place["area"])
    area_r = at("area_r", [32, SEQ], R, place["area"])
    xs = at("xs", [QT, D_MODEL], F, place["area"])
    half = place["area"] + 16 * TILE
    ixw = at("ixw", [KT, KW], F, half)
    ixw_hi = at("ixw_hi", [KT, KW], R, half + 4 * KT * KW)
    ixw_lo = at("ixw_lo", [KT, KW], R, half + 8 * KT * KW)
    stage = at("stage", [2, 2, CW], F, place["stage"])
    w_hi = at("w_hi", [RING, 2, CW], R, place["w_hi"])
    w_lo = at("w_lo", [RING, 2, CW], R, place["w_lo"])

    qh, ql, kh, kl, vh, vl = [at(n, [SEQ], R, work + i * TILE)
                              for i, n in enumerate(["qh", "ql", "kh", "kl", "vh", "vl"])]
    x_hi = at("x_hi", [TRI], R, work + 6 * TILE)
    p_sa = at("p_sa", [TRI], F, work + 6 * TILE)
    x_lo = at("x_lo", [TRI], R, work + 6 * TILE + 4 * TRI)
    w2 = work + 6 * TILE + 8 * TRI
    full = at("full", [2, SEQ], F, w2)
    eb = at("eb", [2, SEQ], F, w2 + 2 * TILE)
    og = at("og", [SEQ], F, w2 + 4 * TILE)
    gain = at("gain", [D_MODEL], F, work)
    junk = at("junk", [D_MODEL], F, work + 4 * TILE)
    xg = at("xg", [QT, D_MODEL], F, place["w_hi"])
    kix_hi = at("kix_hi", [SEQ], R, work)
    kix_lo = at("kix_lo", [SEQ], R, work + TILE)
    kw_t = at("kw_t", [SEQ], F, work + 2 * TILE)
    relu = at("relu", [2, SEQ], F, work + 8 * TILE)
    score = at("score", [2, SEQ], F, work + 10 * TILE)
    dist_i = at("dist_i", [TRI], I, work + 3 * TILE)
    o_first = at("o_first", [4, SEQ], F, w2)
    o_in = at("o_in", [8, SEQ], F, work)
    mix = at("mix", [QT, SEQ], F, work + 8 * TILE)
    mix_sa = at("mix_sa", [SEQ], F, work + 12 * TILE)
    fgain = at("fgain", [D_MODEL], F, place["far"])
    junk2 = at("junk2", [2, CW], F, place["far"] + 4 * D_MODEL)
    assert place["far"] + 4 * D_MODEL + 8 * CW <= top[0]
    last_hi = at("last_hi", [KT - 2 * SHARED, CW], R, place["u_lo"])
    last_lo = at("last_lo", [KT - 2 * SHARED, CW], R, work)

    far = at("far", [TRI], F, place["far"])
    ident = at("ident", [P], F, place["const"])
    big_ident = at("big_ident", [P], R, place["const"] + 4 * P)
    neg_tri = at("neg_tri", [P], R, place["const"] + 8 * P)
    neg_one = at("neg_one", [P], R, place["const"] + 12 * P)
    before = at("before", [P], F, place["const"] + 16 * P)
    cst = at("cst", [2, P], F, w2 + 4 * TILE)

    small_at = [place["small"]]

    def small(name, shape):
        size = 4
        for d in shape:
            size *= d
        small_at[0] += (size + 31) // 32 * 32
        assert small_at[0] <= place["small"] + SMALL
        return at(name, shape, F, small_at[0] - (size + 31) // 32 * 32)

    wix = small("wix", [QT, IDX_HEADS])
    top8 = small("top8", [8])
    ss, var, root, rinv, tmp, rstd = [small(n, [QT]) for n in ("ss", "var", "root", "rinv", "tmp", "rstd")]
    nmax, psum_p, pinv = [small(n, [QT]) for n in ("nmax", "psum_p", "pinv")]
    slope = small("slope", [HEADS])
    ssq = small("ssq", [QT, 4])

    proj = [nc.alloc_psum_tensor(f"proj{i}", [P, CW], F) for i in range(4)]
    attn = [nc.alloc_psum_tensor(f"attn{i}", [P, CW], F) for i in range(4)]

    xt = (attn, proj)
    kw_bank = attn[3]

    o_dram = nc.dram_tensor("o_scratch", (2 * HEADS, P, SEQ), F, kind="Internal").ap()

    win = w_in[0].rearrange("(t p) e -> p t e", p=P)
    wsb = w_branch_sb[0].rearrange("(t p) e -> p t e", p=P)
    wsa = w_branch_sa[0].rearrange("(t p) e -> p t e", p=P)
    wout = w_out[0].rearrange("(t p) e -> p t e", p=P)
    x_rows = x[0].rearrange("(i p) d -> i p d", p=P)
    out_rows = out[0].rearrange("(i p) d -> i p d", p=P)

    def sem(name):
        return nc.alloc_semaphore(name)

    strip_loaded = [sem("strip_loaded0"), sem("strip_loaded1")]
    strip_hi, strip_lo, strip_used = sem("strip_hi"), sem("strip_lo"), sem("strip_used")
    proj_done, proj_free = sem("proj_done"), sem("proj_free")
    x_loaded = [sem(f"x_loaded{i}") for i in range(QT)]
    gain_loaded, ixw_loaded, consts, masks = sem("gain_loaded"), sem("ixw_loaded"), sem("consts"), sem("masks")
    xg_ready, sumsq, norm_step, rooted, xn_ready = sem("xg_ready"), sem("sumsq"), sem("norm_step"), sem("rooted"), sem("xn_ready")
    xt_done, u_hi_ready, u_lo_ready = sem("xt_done"), sem("u_hi_ready"), sem("u_lo_ready")
    ixw_hi_ready, ixw_lo_ready, kw_done, kw_copied = sem("ixw_hi_ready"), sem("ixw_lo_ready"), sem("kw_done"), sem("kw_copied")
    kix_hi_ready, kix_lo_ready = sem("kix_hi_ready"), sem("kix_lo_ready")
    wix_turned, wix_ready, dist_ready, far_ready = sem("wix_turned"), sem("wix_ready"), sem("dist_ready"), sem("far_ready")
    qix_hi_ready = sem("qix_hi_ready")
    dots_done, relu_ready, relu_used, pick_step = sem("dots_done"), sem("relu_ready"), sem("relu_used"), sem("pick_step")
    og_free, qk_hi, qk_lo, v_hi, v_lo = sem("og_free"), sem("qk_hi"), sem("qk_lo"), sem("v_hi"), sem("v_lo")
    z_done, e_step, e_ready, sp_step, sp_ready = sem("z_done"), sem("e_step"), sem("e_ready"), sem("sp_step"), sem("sp_ready")
    sp_hi, sp_lo, c_done = sem("sp_hi"), sem("sp_lo"), sem("c_done")
    w_full, w_low, av_done = sem("w_full"), sem("w_low"), sem("av_done")
    gate_exp, silu_step, o_ready, o_stored = sem("gate_exp"), sem("silu_step"), sem("o_ready"), sem("o_stored")
    lg_ready, max_ready, p_exp, inv_ready, p_ready = sem("lg_ready"), sem("max_ready"), sem("p_exp"), sem("inv_ready"), sem("p_ready")
    pt_done, pt_hi = sem("pt_done"), sem("pt_hi")
    sigmoid_ready = sem("sigmoid_ready")
    o_loaded = [sem(f"o_loaded{i}") for i in range(4)]
    o_first_hi, o_hi, o_lo = sem("o_first_hi"), sem("o_hi"), sem("o_lo")
    branch_sa_done, attn_free, mix_ready, mix_hi, mix_lo = (
        sem("branch_sa_done"), sem("attn_free"), sem("mix_ready"), sem("mix_hi"), sem("mix_lo"))
    res_loaded, fgain_loaded, h_ready, sq_done, y_stored = (
        sem("res_loaded"), sem("fgain_loaded"), sem("h_ready"), sem("sq_done"), sem("y_stored"))
    y_ready = [sem("y_ready_v"), sem("y_ready_s")]
    YV = 1280
    hg_ready, last_done = sem("hg_ready"), sem("last_done")

    SCALE = float(HD) ** -0.5
    HALVES = (slice(0, IDX_DIM), slice(IDX_DIM, P))

    def returned(t):
        return o_first[:, t, :] if t < 4 else o_in[:, (t - 4) % 8, :]

    def bank_done(eng, c, e, strips=NS, done=proj_done, m=None):
        if e < 3:
            eng.wait_ge(done, (c if m is None else m) * 3 + (e + 1))
        else:
            eng.wait_ge(strip_used, c * NS + strips)

    SA_LOOPS = ((0, 4), (4, 6), (6, HEADS))
    V_LOOP = 4

    block = nc.Block()

    with block:
        @block.sync
        def _(sp):
            for i in range(QT):
                sp.dma_start(xs[:, i, :], x_rows[i]).then_inc(x_loaded[i], 16)
                if i == 0:
                    sp.dma_start(gain[:, :], norm_gain[0:1, :].to_broadcast([P, D_MODEL])
                                 ).then_inc(gain_loaded, 16)
            sp.dma_start(ixw[:, :, :], win[:, :, COL_KIX:COL_KIX + KW]).then_inc(ixw_loaded, 16)

            def load_strip(c, s, src):
                if not (isinstance(c, int) and NS * c + s < 2):
                    sp.wait_ge(strip_lo, c * NS + (s - 1))
                sp.dma_start(stage[:, s % 2, :, :], src).then_inc(strip_loaded[s % 2], 16)

            def load_chunk(c, source, col):
                for s in range(NS):
                    load_strip(c, s, source(s)[:, :, ds(col, CW)] if not isinstance(col, int)
                               else source(s)[:, :, col:col + CW])

            def rows(w):
                return lambda s: w[:, 2 * s:2 * s + 2, :]

            def branch_rows(s):
                return (wsb if s < NS // 2 else wsa)[:, 2 * (s % (NS // 2)):2 * (s % (NS // 2)) + 2, :]

            for c in range(C_QIX, C_SB):
                load_chunk(c, rows(win), COL_QIX + CW * c)
            with sp.Fori(C_SB, C_GATE) as c:
                load_chunk(c, rows(win), c * CW + (COL_SB - C_SB * CW))
            with sp.Fori(C_GATE, C_BRANCH) as c:
                load_chunk(c, rows(win), c * CW + (COL_GATE - C_GATE * CW))
            with sp.Fori(C_BRANCH, C_OUT) as c:
                load_chunk(c, branch_rows, c * CW - C_BRANCH * CW)
            with sp.Fori(C_OUT, C_END) as c:
                load_chunk(c, rows(wout), c * CW - C_OUT * CW)
            for i in range(QT):
                for part, cols in enumerate((slice(0, YV), slice(YV, D_MODEL))):
                    sp.wait_ge(y_ready[part], i + 1)
                    sp.dma_start(out_rows[i][:, cols], hres[:, i, cols]).then_inc(y_stored, 16)
            sp.wait_ge(y_stored, 16 * 2 * QT)

        @block.gpsimd
        def _(pool):
            g = nc.gpsimd
            g.memset(ident[:, :], 0.0).then_inc(consts, 1)
            g.memset(before[:, :], 1.0).then_inc(consts, 1)
            g.memset(cst[:, 0, :], 0.0).then_inc(consts, 1)
            g.memset(cst[:, 1, :], -1.0).then_inc(consts, 1)
            pool.wait_ge(consts, 4)
            g.affine_select(out=ident[:, :], in_=ident[:, :], compare_op=ALU.not_equal, fill=1.0,
                            base=0, pattern=[[-1, P]], channel_multiplier=1).then_inc(masks, 1)
            g.affine_select(out=before[:, :], in_=before[:, :], compare_op=ALU.is_gt, fill=0.0,
                            base=0, pattern=[[1, P]], channel_multiplier=-1).then_inc(masks, 1)
            g.affine_select(out=cst[:, 0, :], in_=cst[:, 0, :], compare_op=ALU.is_gt, fill=-1.0,
                            base=0, pattern=[[1, P]], channel_multiplier=-1).then_inc(masks, 1)
            pool.wait_ge(gain_loaded, 16)
            for i in range(2, QT):
                pool.wait_ge(x_loaded[i], 16)
                g.tensor_tensor(xg[:, i, :], xs[:, i, :], gain[:, :], ALU.mult).then_inc(xg_ready, 1)
            pool.wait_ge(ixw_hi_ready, 1)
            g.tensor_tensor(ixw_lo[:, :, :], ixw[:, :, :], ixw_hi[:, :, :].bitcast(F),
                            ALU.subtract).then_inc(ixw_lo_ready, 1)
            pool.wait_ge(sumsq, QT)
            pool.wait_ge(xn_ready, QT)
            for i in range(QT):
                g.iota(dist_i[:, OQ[i]:OQ[i] + WQ[i]], pattern=[[-1, WQ[i]]], base=P * i,
                       channel_multiplier=1).then_inc(dist_ready, 1)

            pool.wait_ge(consts, 5)
            pool.nop(nofuse=True).then_inc(og_free, 1)

            def store_head(hh):
                pool.wait_ge(o_ready, hh + 1)
                pool.dma_start(o_dram[ds(hh, 1)].rearrange("a p s -> p (a s)"), og[:, :]).then_inc(o_stored, 16)
                pool.wait_ge(o_stored, hh * 16 + 16)
                pool.nop(nofuse=True).then_inc(og_free, 1)

            with pool.Fori(0, HEADS) as n:
                store_head(n)

            def outputs_back(j):
                dst = o_first[:, :, :] if j == 0 else o_in[:, 4 * ((j - 1) % 2):4 * ((j - 1) % 2) + 4, :]
                pool.dma_start(dst, o_dram[4 * j:4 * j + 4].rearrange("a p s -> p a s")).then_inc(o_loaded[j], 16)

            outputs_back(0)
            with pool.Fori(HEADS, 2 * HEADS) as hh:
                store_head(hh)
            pool.wait_ge(av_done, 2 * HEADS)
            outputs_back(1)
            outputs_back(2)
            pool.wait_ge(o_lo, 8)
            outputs_back(3)
            pool.wait_ge(strip_used, NS * C_OUT)
            pool.dma_start(hres[:, :, :], x[0].rearrange("(i p) d -> p i d", p=P)).then_inc(res_loaded, 16)
            pool.dma_start(fgain[:, :], final_gain.rearrange("(a d) -> a d", a=1).to_broadcast([P, D_MODEL])
                           ).then_inc(fgain_loaded, 16)

        @block.scalar
        def _(act):
            A = nc.scalar.activation

            def split_hi(c, s):
                act.wait_ge(strip_loaded[s % 2], c * (16 * NS // 2) + 16 * (s // 2 + 1))
                if not (isinstance(c, int) and NS * c + s < RING):
                    act.wait_ge(strip_used, c * NS + (s - RING + 1))
                A(w_hi[:, s % RING, :, :], stage[:, s % 2, :, :], ACT.Copy).then_inc(strip_hi, 1)

            def chunk(c, steps=()):
                for s in range(NS):
                    split_hi(c, s + LEAD)
                    if s < len(steps) and steps[s]:
                        steps[s]()

            def apart():
                act.nop(nofuse=True)

            def evacuate(c, dst):
                for e in range(4):
                    bank_done(act, c, e)
                    apart()
                    A(dst(e), proj[e][:, :], ACT.Copy).then_inc(proj_free, 1)

            def evacuate_rows(c, dst):
                for i in range(QT):
                    bank_done(act, c, i)
                    apart()
                    d = dst(slice(P * i, P * i + P))
                    A(d, proj[i][:, :].rearrange("p (h d) -> p h d", h=4), ACT.Copy).then_inc(proj_free, 1)

            def turned_u_high(i):
                for j in range(4):
                    act.wait_ge(xt_done, 4 * i + j + 1)
                    A(u_hi[:, 4 * j:4 * j + 4, P * i:P * i + P],
                      xt[i % 2][j][:, :].rearrange("p (t s) -> p t s", t=4), ACT.Copy).then_inc(u_hi_ready, 1)

            nc.scalar.preload_act_table_set("sqrt_and_others")
            for i in range(QT):
                act.wait_ge(x_loaded[i], 16)
                if i:
                    act.wait_ge(sumsq, i)
                A(junk[:, :], xs[:, i, :], ACT.Square, accum_out=ss[:, i:i + 1]).then_inc(sumsq, 1)
                if i == 3:
                    turned_u_high(1)
                act.wait_ge(norm_step, 6 * i + 1)
                A(root[:, i:i + 1], var[:, i:i + 1], ACT.Sqrt).then_inc(rooted, 1)
                if i == 1:
                    turned_u_high(0)
            act.wait_ge(ixw_loaded, 16)
            A(ixw_hi[:, :, :], ixw[:, :, :], ACT.Copy).then_inc(ixw_hi_ready, 1)
            turned_u_high(2)
            turned_u_high(3)
            act.wait_ge(xt_done, 4 * QT)
            for s in range(LEAD):
                split_hi(0, s)
            act.wait_ge(kw_done, QT // 2)
            for rows_ in HALVES:
                A(kix_hi[rows_, :], kw_bank[0:IDX_DIM, :], ACT.Copy).then_inc(kix_hi_ready, 1)
            A(kw_t[0:KW, :], kw_bank[0:KW, :], ACT.Copy).then_inc(kw_copied, 1)
            act.wait_ge(dist_ready, QT)
            A(far[:, :], dist_i[:, :], ACT.Abs).then_inc(far_ready, 1)

            nc.scalar.preload_act_table_set("natural_log_exp_and_others")
            for c in range(C_QIX, C_SB):
                chunk(c)
                for e in range(4):
                    bank_done(act, c, e)
                    for par, rows_ in enumerate(HALVES):
                        A(area_r[rows_, 16 + 8 * c + 2 * e + par, :], proj[e][rows_, :],
                          ACT.Copy).then_inc(qix_hi_ready, 1)

            def relu_step(qi, s):
                def f():
                    for h in (2 * s, 2 * s + 1):
                        n = IDX_HEADS * (qi - 1) + h
                        act.wait_ge(dots_done, n + 1)
                        if n >= 2:
                            act.wait_ge(relu_used, n - 1)
                        A(relu[:, n % 2, 0:WQ[qi]], attn[h % 4][:, 0:WQ[qi]], ACT.Relu).then_inc(relu_ready, 1)
                return f

            for c in range(C_SB, C_SB + 4):
                qi = c - C_SB + 1
                chunk(c, [relu_step(qi, s) for s in range(NS - 1)] if qi < QT else ())
                evacuate(c, lambda e: area[:, 4 * (c - C_SB) + e, :])
                if qi < QT:
                    relu_step(qi, NS - 1)()
            with act.Fori(C_SB + 4, C_SB + 6) as c:
                chunk(c)
                evacuate_rows(c, lambda cols: area[:, ds(c * 4 - 4 * C_SB, 4), cols])
            with act.Fori(C_SB + 6, C_SA) as c:
                chunk(c)
                evacuate(c, lambda e: area[:, ds(c * 4 + (e - 4 * C_SB), 1), :])

            def stage_qk(hh, q_slot, k_slot):
                def f():
                    act.wait_ge(strip_used, hh * NS + (NS * C_SA - NS + 3))
                    apart()
                    A(qh[:, :], area[:, ds(q_slot, 1), :], ACT.Copy, scale=SCALE).then_inc(qk_hi, 1)
                    A(kh[:, :], area[:, ds(k_slot, 1), :], ACT.Copy).then_inc(qk_hi, 1)
                return f

            def v_high(v_slot):
                A(vh[:, :], area[:, ds(v_slot, 1), :], ACT.Copy).then_inc(v_hi, 1)

            def gate_exp_z(hh, z_slot):
                act.wait_ge(og_free, hh + 1)
                apart()
                A(og[:, :], area[:, ds(z_slot, 1), :], ACT.Exp, scale=-1.0).then_inc(gate_exp, 1)

            def sb_steps(n):
                def e_tile(i):
                    w = WK[i]
                    act.wait_ge(z_done, n * 4 + i + 1)
                    if i >= 2:
                        act.wait_ge(sp_ready, n * 4 + i - 1)
                    t = eb[:, i % 2, 0:w]
                    A(t, attn[i][:, 0:w], ACT.Abs).then_inc(e_step, 1)
                    act.wait_ge(e_step, n * 8 + 2 * i + 1)
                    A(t, t, ACT.Exp, scale=-1.0).then_inc(e_step, 1)
                    act.wait_ge(e_step, n * 8 + 2 * i + 2)
                    A(t, t, ACT.Ln, bias=1.0).then_inc(e_ready, 1)

                def sp_high(i):
                    act.wait_ge(sp_ready, n * 4 + i + 1)
                    A(x_hi[:, OK[i]:OK[i] + WK[i]], full[:, i % 2, 0:WK[i]], ACT.Copy).then_inc(sp_hi, 1)

                def weights(i):
                    w = WK[i]
                    if i == 0:
                        act.wait_ge(c_done, n * 4 + 4)
                    if i >= 2:
                        act.wait_ge(w_low, n * 4 + i - 1)
                    A(full[:, i % 2, 0:w], attn[i][:, 0:w], ACT.Exp).then_inc(w_full, 1)
                    A(x_hi[:, OK[i]:OK[i] + w], attn[i][:, 0:w], ACT.Exp).then_inc(w_full, 1)

                def s1():
                    v_high(n + 2 * HEADS)
                    e_tile(0)
                    e_tile(1)

                def s2():
                    sp_high(0)
                    e_tile(2)
                    sp_high(1)

                def s3():
                    e_tile(3)
                    sp_high(2)
                    sp_high(3)

                def s5():
                    weights(0)
                    weights(1)

                def s6():
                    weights(2)
                    weights(3)

                return [stage_qk(n, n, n + HEADS), s1, s2, s3,
                        lambda: gate_exp_z(n, n + 3 * HEADS), s5, s6]

            for first, end in SA_LOOPS:
                with act.Fori(first, end) as n:
                    c = n + C_SA
                    chunk(c, sb_steps(n))
                    act.wait_ge(v_lo, n + 1)
                    act.wait_ge(qk_lo, n * 2 + 2)
                    act.wait_ge(silu_step, n * 3 + 3)
                    if first == V_LOOP:
                        evacuate_rows(c, lambda cols: area[:, ds(n, 4, 8), cols])
                    else:
                        evacuate(c, lambda e: area[:, ds(n + 8 * e, 1), :])

            def sa_steps(n, slot):
                hh = n + HEADS

                def probs(i):
                    act.wait_ge(max_ready, n * 4 + i + 1)
                    t = p_sa[:, OQ[i]:OQ[i] + WQ[i]]
                    A(t, t, ACT.Exp, bias=nmax[:, i:i + 1],
                      accum_out=psum_p[:, i:i + 1]).then_inc(p_exp, 1)

                def turned_high(i):
                    if i == 0:
                        act.wait_ge(pt_done, n * 4 + 4)
                    A(x_hi[:, OK[i]:OK[i] + WK[i]], attn[i][:, 0:WK[i]], ACT.Copy).then_inc(pt_hi, 1)

                def s2():
                    probs(0)
                    probs(1)

                def s3():
                    probs(2)
                    probs(3)

                def s5():
                    for i in range(QT):
                        turned_high(i)

                return [stage_qk(hh, slot(0), slot(1)), lambda: v_high(slot(2)), s2, s3,
                        lambda: gate_exp_z(hh, slot(3)), s5]

            with act.Fori(0, 2) as a:
                with act.Fori(0, 4) as b:
                    n = a * 4 + b
                    chunk(n + C_GATE, sa_steps(n, lambda kind: b * 8 + a + 2 * kind))
                    act.wait_ge(v_lo, n + HEADS + 1)
                    act.wait_ge(qk_lo, n * 2 + 2 * HEADS + 2)
                    act.wait_ge(silu_step, n * 3 + 3 * HEADS + 3)
                    evacuate(n + C_GATE, lambda e: area[:, ds(b * 8 + a + 2 * e, 1), :])

            def o_high(ts):
                def f():
                    for t in ts:
                        if t % 4 == 0:
                            act.wait_ge(o_loaded[t // 4], 16)
                        if t == 4:
                            act.wait_ge(strip_used, NS * C_BRANCH)
                        A(u_hi[:, t, :], returned(t), ACT.Copy).then_inc(o_hi, 1)
                return f

            def sigmoid_steps(c):
                def f(e):
                    def g():
                        t = area[:, 8 * (c - C_BRANCH) + 2 * e:8 * (c - C_BRANCH) + 2 * e + 2, :] \
                            if isinstance(c, int) else area[:, ds(c * 8 + (2 * e - 8 * C_BRANCH), 2), :]
                        A(t, t, ACT.Sigmoid).then_inc(sigmoid_ready, 1)
                    return g
                return [f(e) for e in range(4)]

            def mix_high(c):
                for e in range(4):
                    d = c * 4 + (e - 4 * C_BRANCH)
                    act.wait_ge(mix_ready, d + 1)
                    apart()
                    A(area_r[:, ds(d * 2, 1), :], mix[:, e, :], ACT.Copy).then_inc(mix_hi, 1)

            sig = sigmoid_steps(C_BRANCH)
            chunk(C_BRANCH, [o_high(range(4, 8)), o_high(range(8, 12)), sig[0], o_high(range(12, 16)),
                             sig[1], sig[2], sig[3]])
            for e in range(4):
                act.wait_ge(mix_ready, e + 1)
                A(area_r[:, 2 * e, :], mix[:, e, :], ACT.Copy).then_inc(mix_hi, 1)
            with act.Fori(C_BRANCH + 1, C_OUT) as c:
                chunk(c, sigmoid_steps(c))
                mix_high(c)

            def squares(c, tiles=range(QT)):
                m = c - C_OUT
                for i in tiles:
                    act.wait_ge(h_ready, m * 4 + i + 1)
                    src = hres[:, i, CW * m:CW * m + CW] if isinstance(c, int) else hres[:, i, ds(m * CW, CW)]
                    acc = ssq[:, i, m:m + 1] if isinstance(c, int) else ssq[:, i, ds(m, 1)]
                    if 4 * m + i >= 2:
                        act.wait_ge(sq_done, m * 4 + i - 1)
                    A(junk2[:, i % 2, :], src, ACT.Square, accum_out=acc).then_inc(sq_done, 1)

            for c in range(C_OUT, C_LAST):
                chunk(c)
                if c == C_LAST - 1:
                    for s in range(LEAD, SHARED):
                        split_hi(C_LAST, s)
                squares(c)
            for s in range(SHARED, NS):
                t = 2 * (s - SHARED)
                act.wait_ge(strip_loaded[s % 2], 16 * (C_LAST * NS // 2 + s // 2 + 1))
                A(last_hi[:, t:t + 2, :], stage[:, s % 2, :, :], ACT.Copy).then_inc(strip_hi, 1)
            nc.scalar.preload_act_table_set("sqrt_and_others")
            for i in range(QT):
                squares(C_LAST, (i,))
                act.wait_ge(norm_step, 6 * QT + 7 * i + 2)
                A(root[:, i:i + 1], var[:, i:i + 1], ACT.Sqrt).then_inc(rooted, 1)
                act.wait_ge(norm_step, 6 * QT + 7 * i + 7)
                act.wait_ge(hg_ready, 4 * (C_LAST - C_OUT) + i + 1)
                t = hres[:, i, YV:D_MODEL]
                A(t, t, ACT.Copy, scale=rstd[:, i:i + 1]).then_inc(y_ready[1], 1)

        @block.vector
        def _(dve):
            V = nc.vector

            def split_lo(c, s):
                dve.wait_ge(strip_hi, c * NS + (s + 1))
                V.tensor_tensor(w_lo[:, s % RING, :, :], stage[:, s % 2, :, :],
                                w_hi[:, s % RING, :, :].bitcast(F), ALU.subtract).then_inc(strip_lo, 1)

            def chunk(c, steps=()):
                for s in range(NS):
                    split_lo(c, s + LEAD)
                    if s < len(steps) and steps[s]:
                        steps[s]()

            def rsqrt(cols, k, first, between=()):
                between = list(between)

                def step(ins):
                    ins.then_inc(norm_step, 1)
                    if between:
                        between.pop(0)()
                v_, r_, t_, y_, s_ = (t[:, cols] for t in (var, root, tmp, rinv, ss))
                step(V.tensor_scalar(v_, s_, 1.0 / D_MODEL, EPS, ALU.mult, ALU.add))
                dve.wait_ge(rooted, k)
                step(V.reciprocal(y_, r_))
                dve.wait_ge(norm_step, first + 2)
                step(V.tensor_tensor(t_, y_, y_, ALU.mult))
                dve.wait_ge(norm_step, first + 3)
                step(V.tensor_tensor(t_, t_, v_, ALU.mult))
                dve.wait_ge(norm_step, first + 4)
                step(V.tensor_scalar(t_, t_, -0.5, 1.5, ALU.mult, ALU.add))
                dve.wait_ge(norm_step, first + 5)
                step(V.tensor_tensor(rstd[:, cols], y_, t_, ALU.mult))

            for h in range(HEADS):
                V.memset(slope[:, h:h + 1], -(2.0 ** (-8.0 * (h + 1) / HEADS)))
            dve.wait_ge(masks, 3)
            V.tensor_scalar(big_ident[:, :], ident[:, :], BIG, None, ALU.mult)
            V.tensor_copy(neg_tri[:, :], cst[:, 0, :])
            V.tensor_copy(neg_one[:, :], cst[:, 1, :]).then_inc(consts, 1)

            def turned_u_low(i):
                def f(j):
                    def g():
                        dve.wait_ge(u_hi_ready, 4 * i + j + 1)
                        V.tensor_tensor(u_lo[:, 4 * j:4 * j + 4, P * i:P * i + P],
                                        xt[i % 2][j][:, :].rearrange("p (t s) -> p t s", t=4),
                                        u_hi[:, 4 * j:4 * j + 4, P * i:P * i + P].bitcast(F),
                                        ALU.subtract).then_inc(u_lo_ready, 1)
                    return g
                return [f(j) for j in range(4)]

            for i in range(QT):
                dve.wait_ge(sumsq, i + 1)
                rsqrt(slice(i, i + 1), i + 1, 6 * i, turned_u_low(i - 2) if i >= 2 else ())
                dve.wait_ge(norm_step, 6 * i + 6)
                if i < 2:
                    dve.wait_ge(gain_loaded, 16)
                    V.scalar_tensor_tensor(xg[:, i, :], xs[:, i, :], rstd[:, i:i + 1], gain[:, :],
                                           ALU.mult, ALU.mult).then_inc(xn_ready, 1)
                else:
                    dve.wait_ge(xg_ready, i - 1)
                    V.tensor_scalar(xg[:, i, :], xg[:, i, :], rstd[:, i:i + 1], None,
                                    ALU.mult).then_inc(xn_ready, 1)
            for low in turned_u_low(2) + turned_u_low(3):
                low()
            for s in range(LEAD):
                split_lo(0, s)
            dve.wait_ge(kix_hi_ready, 2)
            dve.wait_ge(kw_copied, 1)
            for rows_ in HALVES:
                V.tensor_tensor(kix_lo[rows_, :], kw_bank[0:IDX_DIM, :], kix_hi[0:IDX_DIM, :].bitcast(F),
                                ALU.subtract).then_inc(kix_lo_ready, 1)
            dve.wait_ge(far_ready, 1)
            V.memset(far[0:P // 2, P // 2:P], BIG)
            dve.wait_ge(wix_turned, 1)
            V.tensor_scalar(wix[:, :, :],
                            attn[0][:, 0:QT * KW].rearrange("p (i e) -> p i e", i=QT)[:, :, IDX_DIM:KW],
                            IDX_HEADS ** -0.5 * IDX_DIM ** -0.5, None, ALU.mult).then_inc(wix_ready, 1)

            for c in range(C_QIX, C_SB):
                chunk(c)
                for e in range(4):
                    dve.wait_ge(qix_hi_ready, 8 * c + 2 * e + 2)
                    for par, rows_ in enumerate(HALVES):
                        h = 16 + 8 * c + 2 * e + par
                        m = V.tensor_tensor(area_r[HALVES[1 - par], h, :], proj[e][rows_, :],
                                            area_r[rows_, h, :].bitcast(F), ALU.subtract)
                    m.then_inc(proj_free, 1)

            def score_step(qi, s):
                w = WQ[qi]
                acc = score[:, qi % 2, 0:w]
                for h in (2 * s, 2 * s + 1):
                    n = IDX_HEADS * (qi - 1) + h
                    dve.wait_ge(relu_ready, n + 1)
                    if h == 0:
                        if n == 0:
                            dve.wait_ge(wix_ready, 1)
                        V.tensor_scalar(acc, relu[:, n % 2, 0:w], wix[:, qi, h:h + 1], None,
                                        ALU.mult).then_inc(relu_used, 1)
                    else:
                        dve.wait_ge(relu_used, n)
                        V.scalar_tensor_tensor(acc, relu[:, n % 2, 0:w], wix[:, qi, h:h + 1], acc,
                                               ALU.mult, ALU.add).then_inc(relu_used, 1)
                if s == NS - 1:
                    dve.wait_ge(relu_used, IDX_HEADS * qi)
                    V.memset(score[0:P // 2, qi % 2, w - P // 2:w], HIDDEN).then_inc(pick_step, 1)

            ROUNDS = TOPK // 8
            PICK = 2 * ROUNDS + 2

            def pick_round(qi, r):
                w = WQ[qi]
                acc = score[:, qi % 2, 0:w]
                base = PICK * (qi - 1) + 2 * r + 1
                dve.wait_ge(pick_step, base)
                V.max(top8[:, :], acc).then_inc(pick_step, 1)
                dve.wait_ge(pick_step, base + 1)
                V.match_replace(acc, top8[:, :], acc, TAKEN).then_inc(pick_step, 1)
                if r == ROUNDS - 1:
                    dve.wait_ge(pick_step, base + 2)
                    V.tensor_scalar(acc, acc, TAKEN, BIG, ALU.not_equal, ALU.mult).then_inc(pick_step, 1)
                    dve.wait_ge(pick_step, base + 3)
                    t = far[:, OQ[qi]:OQ[qi] + w]
                    V.tensor_tensor(t, t, acc, ALU.add).then_inc(far_ready, 1)

            for c in range(C_SB, C_SB + 4):
                qi = c - C_SB + 1

                def step(s, qi=qi):
                    def f():
                        if qi >= 2:
                            for r in range(ROUNDS // NS):
                                pick_round(qi - 1, ROUNDS // NS * s + r)
                        if qi < QT:
                            score_step(qi, s)
                    return f

                chunk(c, [step(s) for s in range(NS)])
            with dve.Fori(C_SB + 4, C_SA) as c:
                chunk(c)

            def qk_low(hh, q_slot, k_slot):
                def f():
                    dve.wait_ge(qk_hi, hh * 2 + 2)
                    V.scalar_tensor_tensor(ql[:, :], area[:, ds(q_slot, 1), :], SCALE, qh[:, :].bitcast(F),
                                           ALU.mult, ALU.subtract).then_inc(qk_lo, 1)
                    V.tensor_tensor(kl[:, :], area[:, ds(k_slot, 1), :], kh[:, :].bitcast(F),
                                    ALU.subtract).then_inc(qk_lo, 1)
                return f

            def v_low(hh, v_slot):
                dve.wait_ge(v_hi, hh + 1)
                V.tensor_tensor(vl[:, :], area[:, ds(v_slot, 1), :], vh[:, :].bitcast(F), ALU.subtract).then_inc(v_lo, 1)

            def silu(hh, z_slot):
                dve.wait_ge(gate_exp, hh + 1)
                V.tensor_scalar(og[:, :], og[:, :], 1.0, None, ALU.add).then_inc(silu_step, 1)
                dve.wait_ge(silu_step, hh * 3 + 1)
                V.reciprocal(og[:, :], og[:, :]).then_inc(silu_step, 1)
                dve.wait_ge(silu_step, hh * 3 + 2)
                V.tensor_tensor(og[:, :], og[:, :], area[:, ds(z_slot, 1), :], ALU.mult).then_inc(silu_step, 1)

            def gated(hh):
                dve.wait_ge(av_done, hh + 1)
                dve.wait_ge(silu_step, hh * 3 + 3)
                V.tensor_tensor(og[:, :], attn[0][:, :], og[:, :], ALU.mult).then_inc(o_ready, 1)

            def sb_steps(n):
                def softplus(i):
                    w = WK[i]
                    dve.wait_ge(e_ready, n * 4 + i + 1)
                    if i >= 2:
                        dve.wait_ge(sp_lo, n * 4 + i - 1)
                    V.scalar_tensor_tensor(full[:, i % 2, 0:w], attn[i][:, 0:w], 0.0, eb[:, i % 2, 0:w],
                                           ALU.max, ALU.add).then_inc(sp_step, 1)
                    dve.wait_ge(sp_step, n * 4 + i + 1)
                    t = full[:, i % 2, 0:P]
                    V.tensor_tensor(t, t, before[:, :], ALU.mult).then_inc(sp_ready, 1)

                def sp_low(i):
                    w = WK[i]
                    dve.wait_ge(sp_hi, n * 4 + i + 1)
                    V.tensor_tensor(x_lo[:, OK[i]:OK[i] + w], full[:, i % 2, 0:w],
                                    x_hi[:, OK[i]:OK[i] + w].bitcast(F), ALU.subtract).then_inc(sp_lo, 1)

                def weights_low(i):
                    w = WK[i]
                    dve.wait_ge(w_full, n * 8 + 2 * i + 2)
                    V.tensor_tensor(x_lo[:, OK[i]:OK[i] + w], full[:, i % 2, 0:w],
                                    x_hi[:, OK[i]:OK[i] + w].bitcast(F), ALU.subtract).then_inc(w_low, 1)

                def s1():
                    v_low(n, n + 2 * HEADS)
                    softplus(0)
                    softplus(1)

                def s2():
                    sp_low(0)
                    softplus(2)
                    sp_low(1)

                def s3():
                    softplus(3)
                    sp_low(2)
                    sp_low(3)

                def s5():
                    weights_low(0)
                    weights_low(1)

                def s6():
                    weights_low(2)
                    weights_low(3)

                return [qk_low(n, n, n + HEADS), s1, s2, s3,
                        lambda: silu(n, n + 3 * HEADS), s5, s6, lambda: gated(n)]

            with dve.Fori(0, HEADS) as n:
                chunk(n + C_SA, sb_steps(n))

            def sa_steps(n, slot):
                hh = n + HEADS

                def logits(i):
                    w = WQ[i]
                    t = p_sa[:, OQ[i]:OQ[i] + w]
                    dve.wait_ge(z_done, hh * 4 + i + 1)
                    V.scalar_tensor_tensor(t, far[:, OQ[i]:OQ[i] + w], slope[:, ds(n, 1)], attn[i][:, 0:w],
                                           ALU.mult, ALU.add).then_inc(lg_ready, 1)
                    dve.wait_ge(lg_ready, n * 4 + i + 1)
                    V.tensor_reduce(nmax[:, i:i + 1], t, AX.X, ALU.max, negate=True).then_inc(max_ready, 1)

                def normalize(i):
                    dve.wait_ge(p_exp, n * 4 + i + 1)
                    V.reciprocal(pinv[:, i:i + 1], psum_p[:, i:i + 1]).then_inc(inv_ready, 1)
                    dve.wait_ge(inv_ready, n * 4 + i + 1)
                    t = p_sa[:, OQ[i]:OQ[i] + WQ[i]]
                    V.tensor_scalar(t, t, pinv[:, i:i + 1], None, ALU.mult).then_inc(p_ready, 1)

                def turned_low(i):
                    dve.wait_ge(pt_hi, n * 4 + i + 1)
                    V.tensor_tensor(x_lo[:, OK[i]:OK[i] + WK[i]], attn[i][:, 0:WK[i]],
                                    x_hi[:, OK[i]:OK[i] + WK[i]].bitcast(F), ALU.subtract).then_inc(w_low, 1)

                def s1():
                    v_low(hh, slot(2))
                    logits(0)
                    logits(1)

                def s2():
                    logits(2)
                    logits(3)

                def s3():
                    normalize(0)
                    normalize(1)

                def s4():
                    normalize(2)
                    normalize(3)
                    silu(hh, slot(3))

                def s5():
                    for i in range(QT):
                        turned_low(i)

                return [qk_low(hh, slot(0), slot(1)), s1, s2, s3, s4, s5, None, lambda: gated(hh)]

            dve.wait_ge(far_ready, QT)
            with dve.Fori(0, 2) as a:
                with dve.Fori(0, 4) as b:
                    n = a * 4 + b
                    chunk(n + C_GATE, sa_steps(n, lambda kind: b * 8 + a + 2 * kind))

            def o_low(ts):
                def f():
                    for t in ts:
                        dve.wait_ge(o_hi, t - 3)
                        V.tensor_tensor(u_lo[:, t, :], returned(t), u_hi[:, t, :].bitcast(F),
                                        ALU.subtract).then_inc(o_lo, 1)
                return f

            def slot_of(c, e, lo):
                if isinstance(c, int):
                    return slice(8 * (c - C_BRANCH) + 2 * e + lo, 8 * (c - C_BRANCH) + 2 * e + lo + 1)
                return ds(c * 8 + (2 * e + lo - 8 * C_BRANCH), 1)

            def mix_sb(c):
                m = c - C_BRANCH

                def f():
                    for e in range(4):
                        bank_done(dve, c, e, strips=NS // 2)
                        dve.wait_ge(sigmoid_ready, m * 4 + e + 1)
                        V.tensor_tensor(mix[:, e, :], proj[e][:, :], area[:, slot_of(c, e, 0), :],
                                        ALU.mult).then_inc(proj_free, 1)
                return f

            def mix_both(c):
                m = c - C_BRANCH
                for e in range(4):
                    bank_done(dve, c, e, done=branch_sa_done, m=m)
                    if not (isinstance(c, int) and e == 0):
                        dve.wait_ge(mix_ready, m * 4 + e)
                    V.tensor_tensor(mix_sa[:, :], attn[e][:, :], area[:, slot_of(c, e, 1), :],
                                    ALU.mult).then_inc(attn_free, 1)
                    dve.wait_ge(attn_free, m * 4 + e + 1)
                    if e == 0:
                        dve.wait_ge(proj_free, c * 4 + 4)
                    V.tensor_tensor(mix[:, e, :], mix[:, e, :], mix_sa[:, :], ALU.add).then_inc(mix_ready, 1)
                for e in range(4):
                    dve.wait_ge(mix_hi, m * 4 + e + 1)
                    V.tensor_tensor(area_r[:, slot_of(c, e, 1), :], mix[:, e, :],
                                    area_r[:, slot_of(c, e, 0), :].bitcast(F), ALU.subtract).then_inc(mix_lo, 1)

            dve.wait_ge(o_loaded[0], 16)
            for t in range(4):
                if t % 2 == 0:
                    dve.wait_ge(strip_used, NS * (C_BRANCH - 1) + t // 2 + 1)
                V.tensor_copy(u_hi[:, t, :], returned(t)).then_inc(o_first_hi, 1)
                dve.wait_ge(o_first_hi, t + 1)
                V.tensor_tensor(u_lo[:, t, :], returned(t), u_hi[:, t, :].bitcast(F),
                                ALU.subtract).then_inc(o_lo, 1)
            chunk(C_BRANCH, [o_low(range(4, 8)), o_low(range(8, 12)), None, o_low(range(12, 16)),
                             None, mix_sb(C_BRANCH)])
            mix_both(C_BRANCH)
            with dve.Fori(C_BRANCH + 1, C_OUT) as c:
                chunk(c, [None, None, None, None, None, mix_sb(c)])
                mix_both(c)

            def residual(c, tiles=range(QT), done=bank_done):
                m = c - C_OUT
                sl = slice(CW * m, CW * m + CW)
                for i in tiles:
                    t = hres[:, i, sl]
                    done(dve, c, i)
                    V.tensor_tensor(t, proj[i][:, :], t, ALU.add).then_inc(h_ready, 1)
                for i in tiles:
                    t = hres[:, i, sl]
                    dve.wait_ge(sq_done, m * 4 + i + 1)
                    V.tensor_tensor(t, t, fgain[:, sl], ALU.mult).then_inc(hg_ready, 1)

            for c in range(C_OUT, C_LAST):
                chunk(c)
                if c == C_LAST - 1:
                    for s in range(LEAD, SHARED):
                        split_lo(C_LAST, s)
                if c == C_OUT:
                    dve.wait_ge(res_loaded, 16)
                    dve.wait_ge(fgain_loaded, 16)
                residual(c)
            for s in range(SHARED, NS):
                t = 2 * (s - SHARED)
                dve.wait_ge(strip_hi, NS * C_LAST + s + 1)
                V.tensor_tensor(last_lo[:, t:t + 2, :], stage[:, s % 2, :, :],
                                last_hi[:, t:t + 2, :].bitcast(F), ALU.subtract).then_inc(strip_lo, 1)
            for i in range(QT):
                residual(C_LAST, (i,), lambda eng, c, i: eng.wait_ge(last_done, i + 1))
                V.tensor_reduce(ss[:, i:i + 1], ssq[:, i, :], AX.X, ALU.add).then_inc(norm_step, 1)
                dve.wait_ge(norm_step, 6 * QT + 7 * i + 1)
                rsqrt(slice(i, i + 1), QT + i + 1, 6 * QT + 7 * i + 1)
                dve.wait_ge(norm_step, 6 * QT + 7 * i + 7)
                dve.wait_ge(hg_ready, 4 * (C_LAST - C_OUT) + i + 1)
                t = hres[:, i, 0:YV]
                V.tensor_scalar(t, t, rstd[:, i:i + 1], None, ALU.mult).then_inc(y_ready[0], 1)

        @block.tensor
        def _(pe):
            def mm3(out_, a_hi, a_lo, b_hi, b_lo, start, stop, free=False):
                nc.tensor.matmul(out_, a_hi, b_hi, start=start, stop=False, skip_group_check=free)
                nc.tensor.matmul(out_, a_hi, b_lo, start=False, stop=False, skip_group_check=free)
                return nc.tensor.matmul(out_, a_lo, b_hi, start=False, stop=stop, skip_group_check=free)

            def strip(c, s, first, last, tokens=None, banks=proj, free_of=None, done=proj_done,
                      ready=None):
                pe.wait_ge(strip_lo, c * NS + (s + 1))
                if ready:
                    ready(2 * s + 1)
                for e in range(4):
                    for j in range(2):
                        t = 2 * s + j
                        st, en = first and j == 0, last and j == 1
                        if st and free_of is not None:
                            free_of(e)
                        cols = slice(P * e, P * e + P)
                        r = s % RING
                        if tokens == "u":
                            m = mm3(banks[e][:, :], u_hi[:, t, cols], u_lo[:, t, cols],
                                    w_hi[:, r, j, :], w_lo[:, r, j, :], st, en)
                        elif tokens == "mixed":
                            m = mm3(banks[e][:, :], area_r[:, 2 * t, cols], area_r[:, 2 * t + 1, cols],
                                    w_hi[:, r, j, :], w_lo[:, r, j, :], st, en)
                        else:
                            m = mm3(banks[e][:, :], w_hi[:, r, j, cols], w_lo[:, r, j, cols],
                                    u_hi[:, t, :], u_lo[:, t, :], st, en)
                        if en and e < 3:
                            m.then_inc(done, 1)
                m.then_inc(strip_used, 1)

            def chunk(c, steps=(), tokens=None, ready=None):
                def bank_free(e):
                    if tokens == "mixed" and not isinstance(c, int):
                        pe.wait_ge(h_ready, c * 4 + (e - 3 - 4 * C_OUT))
                    elif not (isinstance(c, int) and c == 0):
                        pe.wait_ge(proj_free, c * 4 + (e - 3))
                for s in range(NS):
                    strip(c, s, s == 0, s == NS - 1, tokens, free_of=bank_free, ready=ready)
                    if s < len(steps) and steps[s]:
                        steps[s]()

            def turn_x(i):
                pe.wait_ge(xn_ready, i + 1)
                for j in range(4):
                    if i >= 2:
                        pe.wait_ge(u_lo_ready, 4 * (i - 2) + j + 1)
                    for t in range(4):
                        k = 4 * j + t
                        m = nc.tensor.transpose(xt[i % 2][j][:, P * t:P * t + P], xg[:, i, P * k:P * k + P], ident[:, :])
                    m.then_inc(xt_done, 1)

            def index_keys(i):
                cols = slice(P * i, P * i + 2 * P)
                for t in range(KT):
                    if i > 0 and t % 4 == 0:
                        pe.wait_ge(u_lo_ready, 4 * (i + 1) + t // 4 + 1)
                    m = mm3(kw_bank[0:KW, cols], ixw_hi[:, t, :], ixw_lo[:, t, :],
                            u_hi[:, t, cols], u_lo[:, t, cols], t == 0, t == KT - 1)
                m.then_inc(kw_done, 1)

            pe.wait_ge(masks, 1)
            for i in range(QT):
                turn_x(i)
            pe.wait_ge(ixw_lo_ready, 1)
            pe.wait_ge(u_lo_ready, 4 * (QT - 1))
            for i in range(0, QT, 2):
                index_keys(i)

            def turn_wix():
                pe.wait_ge(kw_copied, 1)
                for i in range(QT):
                    m = nc.tensor.transpose(attn[0][:, KW * i:KW * i + KW], kw_t[0:KW, P * i:P * i + P],
                                            ident[0:KW, 0:KW])
                m.then_inc(wix_turned, 1)

            chunk(C_QIX, [turn_wix])
            for c in range(C_QIX + 1, C_SB):
                chunk(c)

            def dots(qi, s):
                def f():
                    for h in (2 * s, 2 * s + 1):
                        n = IDX_HEADS * (qi - 1) + h
                        if n == 0:
                            pe.wait_ge(kix_lo_ready, 2)
                            pe.wait_ge(wix_ready, 1)
                            pe.wait_ge(proj_free, 4 * C_SB)
                        if n >= 4:
                            pe.wait_ge(relu_ready, n - 3)
                        q = area_r[:, 16 + h, P * qi:P * qi + P]
                        o_ = attn[h % 4][:, 0:WQ[qi]]
                        nc.tensor.matmul(o_, q, kix_lo[:, 0:WQ[qi]], start=True, stop=False)
                        nc.tensor.matmul(o_, q, kix_hi[:, 0:WQ[qi]], start=False, stop=True).then_inc(dots_done, 1)
                return f

            for c in range(C_SB, C_SB + 4):
                qi = c - C_SB + 1
                chunk(c, [dots(qi, s) for s in range(NS)] if qi < QT else ())
            with pe.Fori(C_SB + 4, C_SB + 6) as c:
                chunk(c, tokens="u")
            with pe.Fori(C_SB + 6, C_SA) as c:
                chunk(c)

            def times_v(hh):
                pe.wait_ge(v_lo, hh + 1)
                pe.wait_ge(w_low, hh * 4 + 4)
                for i in range(QT):
                    k = slice(OK[i], OK[i] + WK[i])
                    v = slice(P * i, P * i + P)
                    m = mm3(attn[0][:, P * i:SEQ], vh[:, v], vl[:, v], x_hi[:, k], x_lo[:, k],
                            i == 0, i == QT - 1)
                m.then_inc(av_done, 1)

            def sb_steps(n):
                def z(i):
                    k = slice(P * i, P * i + P)
                    mm3(attn[i][:, 0:WK[i]], kh[:, k], kl[:, k], qh[:, P * i:SEQ], ql[:, P * i:SEQ],
                        True, True, True).then_inc(z_done, 1)

                def s0():
                    pe.wait_ge(qk_lo, n * 2 + 2)
                    for i in range(QT):
                        z(i)

                def s4():
                    pe.wait_ge(sp_lo, n * 4 + 4)
                    for i in range(QT):
                        for j in range(i, QT):
                            o_ = attn[i][:, P * (j - i):WK[i]]
                            a = neg_tri if i == j else neg_one
                            for part in (x_lo, x_hi):
                                nc.tensor.matmul(o_, a[:, :], part[:, OK[j]:OK[j] + WK[j]],
                                                 start=False, stop=False, skip_group_check=True)
                        nc.tensor.matmul(attn[i][:, 0:P], big_ident[:, :], neg_tri[:, :], start=False, stop=True,
                                         skip_group_check=True).then_inc(c_done, 1)

                return [s0, None, None, None, s4, None, lambda: times_v(n)]

            pe.wait_ge(consts, 5)
            for first, end in SA_LOOPS:
                with pe.Fori(first, end) as n:
                    chunk(n + C_SA, sb_steps(n), tokens="u" if first == V_LOOP else None)

            def sa_steps(n):
                hh = n + HEADS

                def lg(i):
                    q = slice(P * i, P * i + P)
                    mm3(attn[i][:, 0:WQ[i]], qh[:, q], ql[:, q], kh[:, 0:WQ[i]], kl[:, 0:WQ[i]],
                        True, True).then_inc(z_done, 1)

                def s0():
                    pe.wait_ge(qk_lo, hh * 2 + 2)
                    for i in range(QT):
                        lg(i)

                def s4():
                    pe.wait_ge(p_ready, n * 4 + 4)
                    for i in range(QT):
                        for q in range(i, QT):
                            m = nc.tensor.transpose(attn[i][:, P * (q - i):P * (q - i) + P],
                                                    p_sa[:, OQ[q] + P * i:OQ[q] + P * i + P], ident[:, :])
                        m.then_inc(pt_done, 1)

                return [s0, None, None, None, s4, None, lambda: times_v(hh)]

            with pe.Fori(0, 2) as a:
                with pe.Fori(0, 4) as b:
                    n = a * 4 + b
                    chunk(n + C_GATE, sa_steps(n))

            def branch_chunk(c):
                m_ = c - C_BRANCH

                def sb_free(e):
                    pe.wait_ge(proj_free, c * 4 + (e - 3))

                def sa_free(e):
                    if isinstance(c, int):
                        pe.wait_ge(o_ready, 2 * HEADS)
                    else:
                        pe.wait_ge(attn_free, m_ * 4 + (e - 3))

                ready = (lambda t: pe.wait_ge(o_lo, t + 1)) if isinstance(c, int) else None
                for s in range(NS):
                    h = NS // 2
                    if s < h:
                        strip(c, s, s == 0, s == h - 1, free_of=sb_free, ready=ready)
                    else:
                        strip(c, s, s == h, s == NS - 1, banks=attn, free_of=sa_free, done=branch_sa_done,
                              ready=ready)

            branch_chunk(C_BRANCH)
            with pe.Fori(C_BRANCH + 1, C_OUT) as c:
                branch_chunk(c)

            chunk(C_OUT, tokens="mixed", ready=lambda t: pe.wait_ge(mix_lo, t + 1))
            with pe.Fori(C_OUT + 1, C_LAST) as c:
                chunk(c, tokens="mixed")
            for s in range(SHARED):
                strip(C_LAST, s, s == 0, False, tokens="mixed",
                      free_of=lambda e: pe.wait_ge(h_ready, 4 * (C_LAST - 1 - C_OUT) + e + 1))
            for i in range(QT):
                for t in range(2 * SHARED, KT):
                    if i == 0 and t % 2 == 0:
                        pe.wait_ge(strip_lo, NS * C_LAST + t // 2 + 1)
                    cols = slice(P * i, P * i + P)
                    m = mm3(proj[i][:, :], area_r[:, 2 * t, cols], area_r[:, 2 * t + 1, cols],
                            last_hi[:, t - 2 * SHARED, :], last_lo[:, t - 2 * SHARED, :], False, t == KT - 1)
                m.then_inc(last_done, 1)


_INS = ["x", "norm_gain", "w_in", "w_branch_sb", "w_branch_sa", "w_out", "final_norm_gain"]


def kernel(**inputs):
    import numpy as np
    import concourse.bacc as bacc
    from concourse.bass_utils import run_bass_kernel_spmd

    nc = bacc.Bacc("TRN2", target_bir_lowering=False, num_devices=1,
                   dynamic_dma_scratch_size=8192)
    arrays, args = {}, []
    for name in _INS:
        a = np.ascontiguousarray(inputs[name])
        arrays[f"in_{name}"] = a
        args.append(nc.dram_tensor(f"in_{name}", a.shape, mybir.dt.from_np(a.dtype), kind="ExternalInput").ap())
    args.append(nc.dram_tensor("out_h", (1, SEQ, D_MODEL), mybir.dt.float32, kind="ExternalOutput").ap())
    build(nc, *args)
    r = run_bass_kernel_spmd(nc, [arrays], core_ids=[0])
    return r.results[0]["out_h"]
```
